# Optimizing a Trainium2 kernel written in Bass

```python
import math
import jax, jax.numpy as jnp
from jax import lax
import numpy as np
import jax
import jax.numpy as jnp

D_MODEL = 1024
BATCH = 1
SEQ = 512
DEPTH = 1

D_MIX = D_MODEL
ATT_WIDTH = D_MIX // 2
POOL_WIDTH = D_MIX - ATT_WIDTH
HEAD_DIM = 64
N_HEADS = ATT_WIDTH // HEAD_DIM
IDX_HEADS = 4
IDX_DIM = 64
IDX_ROPE_DIM = 32
INDEX_TOPK = 256
POOL_WINDOWS = (2, 4, 8, 16)
N_POOL_GROUPS = len(POOL_WINDOWS)
POOL_CH = POOL_WIDTH // N_POOL_GROUPS
D_FF = 2816
ROPE_THETA = 10000.0
NORM_EPS = 1e-6
Q_BLOCK = 128
IN_SPLITS = (ATT_WIDTH, ATT_WIDTH, ATT_WIDTH, IDX_HEADS * IDX_DIM, IDX_DIM, IDX_HEADS, POOL_WIDTH)
IN_COLS = sum(IN_SPLITS)


def rms_norm(x, g):
    xf = x.astype(jnp.float32)
    y = xf * lax.rsqrt(jnp.mean(xf * xf, axis=-1, keepdims=True) + NORM_EPS)
    return (y * g.astype(jnp.float32)).astype(x.dtype)

def rope(x, pos, rot_dim):
    half = rot_dim // 2
    inv = ROPE_THETA ** (-jnp.arange(half, dtype=jnp.float32) / half)
    ang = pos.astype(jnp.float32)[:, None] * inv[None, :]
    cos = jnp.cos(ang)[:, None, :]
    sin = jnp.sin(ang)[:, None, :]
    xr = x[..., :rot_dim].astype(jnp.float32)
    x1, x2 = xr[..., :half], xr[..., half:]
    rot = jnp.concatenate([x1 * cos - x2 * sin, x2 * cos + x1 * sin], axis=-1).astype(x.dtype)
    return jnp.concatenate([rot, x[..., rot_dim:]], axis=-1)

def swiglu(x, w_gate, w_up, w_down):
    return (jax.nn.silu(x @ w_gate) * (x @ w_up)) @ w_down

def dsa_attention(q, k, v, q_idx, k_idx, w_idx, top_k):
    B, S, H, Dh = q.shape
    nb = S // Q_BLOCK
    key_pos = jnp.arange(S)
    scale = Dh ** -0.5

    def to_blocks(a):
        return a.reshape((B, nb, Q_BLOCK) + a.shape[2:]).swapaxes(0, 1)

    def block(args):
        qb, qib, wb, posb = args
        rel = jax.nn.relu(jnp.einsum('bthd,bsd->bths', qib, k_idx).astype(jnp.float32))
        score = jnp.einsum('bth,bths->bts', wb.astype(jnp.float32), rel)
        causal = key_pos[None, :] <= posb[:, None]
        score = jnp.where(causal[None], score, -jnp.inf)
        _, idx = lax.top_k(score, top_k)
        valid = idx <= posb[None, :, None]
        k_sel = jax.vmap(lambda kk, ii: kk[ii])(k, idx)
        v_sel = jax.vmap(lambda vv, ii: vv[ii])(v, idx)
        logits = jnp.einsum('bthd,btkhd->bhtk', qb, k_sel).astype(jnp.float32) * scale
        logits = jnp.where(valid[:, None], logits, -jnp.inf)
        p = jax.nn.softmax(logits, axis=-1).astype(v.dtype)
        return jnp.einsum('bhtk,btkhd->bthd', p, v_sel)

    pos_blocks = jnp.arange(S).reshape(nb, Q_BLOCK)
    out = lax.map(block, (to_blocks(q), to_blocks(q_idx), to_blocks(w_idx), pos_blocks))
    return out.swapaxes(0, 1).reshape(B, S, H * Dh)

def multiscale_pool(u):
    B, S, _ = u.shape
    uf = u.astype(jnp.float32).reshape(B, S, N_POOL_GROUPS, POOL_CH)
    c = jnp.concatenate([jnp.zeros((B, 1, N_POOL_GROUPS, POOL_CH), jnp.float32),
                         jnp.cumsum(uf, axis=1)], axis=1)
    t = jnp.arange(S)
    outs = []
    for g, w in enumerate(POOL_WINDOWS):
        cg = c[:, :, g]
        c_lo = jnp.concatenate([jnp.zeros((B, w - 1, POOL_CH), jnp.float32), cg[:, :S + 1 - w]], axis=1)
        count = jnp.minimum(t + 1, w).astype(jnp.float32)[None, :, None]
        outs.append((cg[:, 1:] - c_lo) / count - uf[:, :, g])
    return jnp.stack(outs, axis=2).astype(u.dtype)

def first_inputs(seed: int = 0) -> dict:
    key = jax.random.key(seed)
    ks = jax.random.split(key, 20)
    f32 = jnp.float32

    def nrm(k, shape, fan_in):
        return jax.random.normal(k, shape, f32) * fan_in ** -0.5

    def gain(k, shape):
        return 1.0 + 0.02 * jax.random.normal(k, shape, f32)

    L = DEPTH
    return {
        "x": jax.random.normal(ks[0], (BATCH, SEQ, D_MODEL), f32),
        "ffn1_norm": gain(ks[1], (L, D_MODEL)),
        "ffn1_w_gate": nrm(ks[2], (L, D_MODEL, D_FF), D_MODEL),
        "ffn1_w_up": nrm(ks[3], (L, D_MODEL, D_FF), D_MODEL),
        "ffn1_w_down": nrm(ks[4], (L, D_FF, D_MODEL), D_FF),
        "mix_norm": gain(ks[5], (L, D_MODEL)),
        "w_in": nrm(ks[6], (L, D_MODEL, IN_COLS), D_MODEL),
        "q_norm": gain(ks[7], (L, HEAD_DIM)),
        "k_norm": gain(ks[8], (L, HEAD_DIM)),
        "pool_w": nrm(ks[9], (L, N_POOL_GROUPS, POOL_CH, POOL_CH), POOL_CH),
        "pool_scale": 0.5 + 0.05 * jax.random.normal(ks[10], (L, POOL_WIDTH), f32),
        "w_out": nrm(ks[11], (L, D_MIX, D_MODEL), D_MIX),
        "ffn2_norm": gain(ks[12], (L, D_MODEL)),
        "ffn2_w_gate": nrm(ks[13], (L, D_MODEL, D_FF), D_MODEL),
        "ffn2_w_up": nrm(ks[14], (L, D_MODEL, D_FF), D_MODEL),
        "ffn2_w_down": nrm(ks[15], (L, D_FF, D_MODEL), D_FF),
    }

def first_block(x, ffn1_norm, ffn1_w_gate, ffn1_w_up, ffn1_w_down, mix_norm, w_in,
              q_norm, k_norm, pool_w, pool_scale, w_out,
              ffn2_norm, ffn2_w_gate, ffn2_w_up, ffn2_w_down):
    B, S, _ = x.shape
    top_k = min(INDEX_TOPK, S // 4)
    pos = jnp.arange(S)
    split_points = list(np.cumsum(IN_SPLITS)[:-1])
    idx_scale = (IDX_HEADS ** -0.5) * (IDX_DIM ** -0.5)

    for l in range(DEPTH):
        x = x + 0.5 * swiglu(rms_norm(x, ffn1_norm[l]), ffn1_w_gate[l], ffn1_w_up[l], ffn1_w_down[l])

        h = rms_norm(x, mix_norm[l])
        proj = h @ w_in[l]
        q, k, v, qi, ki, wi, u = jnp.split(proj, split_points, axis=-1)
        q = rope(rms_norm(q.reshape(B, S, N_HEADS, HEAD_DIM), q_norm[l]), pos, HEAD_DIM)
        k = rope(rms_norm(k.reshape(B, S, N_HEADS, HEAD_DIM), k_norm[l]), pos, HEAD_DIM)
        v = v.reshape(B, S, N_HEADS, HEAD_DIM)
        qi = rope(qi.reshape(B, S, IDX_HEADS, IDX_DIM), pos, IDX_ROPE_DIM)
        ki = rope(ki.reshape(B, S, 1, IDX_DIM), pos, IDX_ROPE_DIM)[:, :, 0]
        wi = wi * idx_scale

        attn = dsa_attention(q, k, v, qi, ki, wi, top_k)

        pooled = jnp.einsum('bsgc,gcd->bsgd', multiscale_pool(u), pool_w[l])
        pooled = pooled.reshape(B, S, POOL_WIDTH) * pool_scale[l]

        x = x + jnp.concatenate([attn, pooled], axis=-1) @ w_out[l]

        x = x + 0.5 * swiglu(rms_norm(x, ffn2_norm[l]), ffn2_w_gate[l], ffn2_w_up[l], ffn2_w_down[l])
    return x


GRID_W = 64
CTX_LEN = 256
A_HEADS = 8
A_KV_HEADS = 2
A_GROUPS = A_HEADS // A_KV_HEADS
B_HEADS = 8
B_KV_HEADS = 2
B_GROUPS = B_HEADS // B_KV_HEADS
WINDOW = 128
BLOCK = 128
CONV_WIDTH = 3
LN_EPS = 1e-5
QK_EPS = 1e-6
N_MOD = 6
DEEPNORM_ALPHA = (2.0 * DEPTH) ** 0.25
DEEPNORM_BETA = (8.0 * DEPTH) ** -0.25

OFF_QA = 0
OFF_KA = OFF_QA + A_HEADS * HEAD_DIM
OFF_VA = OFF_KA + A_KV_HEADS * HEAD_DIM
OFF_QB = OFF_VA + A_KV_HEADS * HEAD_DIM
OFF_KB = OFF_QB + B_HEADS * HEAD_DIM
OFF_VB = OFF_KB + B_KV_HEADS * HEAD_DIM
OFF_GA = OFF_VB + B_KV_HEADS * HEAD_DIM
OFF_GB = OFF_GA + D_MODEL
IN_COLS_2 = OFF_GB + D_MODEL


def _layer_norm(x, g, b):
    xf = x.astype(jnp.float32)
    mu = jnp.mean(xf, axis=-1, keepdims=True)
    var = jnp.mean(jnp.square(xf - mu), axis=-1, keepdims=True)
    return ((xf - mu) * lax.rsqrt(var + LN_EPS) * g + b).astype(x.dtype)

def _qk_rms(t, g):
    tf = t.astype(jnp.float32)
    return (tf * lax.rsqrt(jnp.mean(tf * tf, axis=-1, keepdims=True) + QK_EPS) * g).astype(t.dtype)

def _axial_rope_tables(n_tok, dtype):
    pos = jnp.arange(n_tok, dtype=jnp.int32)
    rows = (pos // GRID_W).astype(jnp.float32)
    cols = (pos % GRID_W).astype(jnp.float32)
    n_freq = HEAD_DIM // 4
    inv_freq = ROPE_THETA ** (-jnp.arange(n_freq, dtype=jnp.float32) / n_freq)
    ang_r = rows[:, None, None] * inv_freq
    ang_c = cols[:, None, None] * inv_freq
    return (jnp.cos(ang_r).astype(dtype), jnp.sin(ang_r).astype(dtype),
            jnp.cos(ang_c).astype(dtype), jnp.sin(ang_c).astype(dtype))

def _rotate_half(t, cos, sin):
    t1, t2 = jnp.split(t, 2, axis=-1)
    return jnp.concatenate([t1 * cos - t2 * sin, t2 * cos + t1 * sin], axis=-1)

def _rope_2d(t, tables):
    cos_r, sin_r, cos_c, sin_c = tables
    t_row, t_col = jnp.split(t, 2, axis=-1)
    return jnp.concatenate([_rotate_half(t_row, cos_r, sin_r), _rotate_half(t_col, cos_c, sin_c)], axis=-1)

def _gqa_scores(q, k):
    return jnp.einsum("bqhgd,bkhd->bhgqk", q, k).astype(jnp.float32) * (HEAD_DIM ** -0.5)

def _gqa_values(p, v):
    return jnp.einsum("bhgqk,bkhd->bqhgd", p.astype(v.dtype), v)

def _sink_softmax(scores, sink):
    sink = sink.astype(jnp.float32)[:, :, None, None]
    m = jnp.maximum(jnp.max(scores, axis=-1, keepdims=True), sink)
    e = jnp.exp(scores - m)
    return e / (jnp.sum(e, axis=-1, keepdims=True) + jnp.exp(sink - m))

def _windowed_attention(q, k, v, k_ctx, v_ctx, sink):
    bsz, n_tok = q.shape[:2]
    pad = ((0, 0), (BLOCK, BLOCK), (0, 0), (0, 0))
    k_pad = jnp.pad(k, pad)
    v_pad = jnp.pad(v, pad)
    ctx_mask = jnp.ones((BLOCK, k_ctx.shape[1]), dtype=bool)

    def one_block(i):
        start = i * BLOCK
        q_blk = lax.dynamic_slice_in_dim(q, start, BLOCK, axis=1)
        k_blk = jnp.concatenate([lax.dynamic_slice_in_dim(k_pad, start, 3 * BLOCK, axis=1), k_ctx], axis=1)
        v_blk = jnp.concatenate([lax.dynamic_slice_in_dim(v_pad, start, 3 * BLOCK, axis=1), v_ctx], axis=1)
        q_pos = start + jnp.arange(BLOCK)
        k_pos = start - BLOCK + jnp.arange(3 * BLOCK)
        band = ((jnp.abs(q_pos[:, None] - k_pos[None, :]) <= WINDOW)
                & (k_pos[None, :] >= 0) & (k_pos[None, :] < n_tok))
        mask = jnp.concatenate([band, ctx_mask], axis=1)
        scores = jnp.where(mask, _gqa_scores(q_blk, k_blk), -jnp.inf)
        return _gqa_values(_sink_softmax(scores, sink), v_blk)

    out = lax.map(one_block, jnp.arange(n_tok // BLOCK))
    return jnp.moveaxis(out, 0, 1).reshape(bsz, n_tok, -1)

def _global_attention(q, k_all, v_all):
    bsz, n_tok = q.shape[:2]

    def one_block(i):
        q_blk = lax.dynamic_slice_in_dim(q, i * BLOCK, BLOCK, axis=1)
        p = jax.nn.softmax(_gqa_scores(q_blk, k_all), axis=-1)
        return _gqa_values(p, v_all)

    out = lax.map(one_block, jnp.arange(n_tok // BLOCK))
    return jnp.moveaxis(out, 0, 1).reshape(bsz, n_tok, -1)

def _merge_branches(o_a, o_b, gate_logits, w_branch_a, w_branch_b, w_out):
    g_a, g_b = jnp.split(jax.nn.sigmoid(gate_logits), 2, axis=-1)
    return (g_a * (o_a @ w_branch_a) + g_b * (o_b @ w_branch_b)) @ w_out

def _context_kv(h_c, w_in, b_in, k_norm_g):
    bsz, n_ctx, _ = h_c.shape
    kv_a = (h_c @ w_in[:, OFF_KA:OFF_QB] + b_in[OFF_KA:OFF_QB]).reshape(bsz, n_ctx, 2 * A_KV_HEADS, HEAD_DIM)
    kv_b = (h_c @ w_in[:, OFF_KB:OFF_GA] + b_in[OFF_KB:OFF_GA]).reshape(bsz, n_ctx, 2 * B_KV_HEADS, HEAD_DIM)
    k_a, v_a = jnp.split(kv_a, 2, axis=2)
    k_b, v_b = jnp.split(kv_b, 2, axis=2)
    return (k_a, v_a, _qk_rms(k_b, k_norm_g), v_b)

def _latent_token_mixer(h, kv_ctx, w_in, b_in, sink, q_norm_g, k_norm_g,
                        w_branch_a, w_branch_b, w_out, rope):
    bsz, n_tok, _ = h.shape
    k_a_c, v_a_c, k_b_c, v_b_c = kv_ctx
    proj = h @ w_in + b_in

    def heads(lo, hi, n):
        return proj[..., lo:hi].reshape(bsz, n_tok, n, HEAD_DIM)

    q_a = _rope_2d(heads(OFF_QA, OFF_KA, A_HEADS), rope).reshape(bsz, n_tok, A_KV_HEADS, A_GROUPS, HEAD_DIM)
    k_a = _rope_2d(heads(OFF_KA, OFF_VA, A_KV_HEADS), rope)
    v_a = heads(OFF_VA, OFF_QB, A_KV_HEADS)
    q_b = _rope_2d(_qk_rms(heads(OFF_QB, OFF_KB, B_HEADS), q_norm_g), rope).reshape(
        bsz, n_tok, B_KV_HEADS, B_GROUPS, HEAD_DIM)
    k_b = _rope_2d(_qk_rms(heads(OFF_KB, OFF_VB, B_KV_HEADS), k_norm_g), rope)
    v_b = heads(OFF_VB, OFF_GA, B_KV_HEADS)
    o_a = _windowed_attention(q_a, k_a, v_a, k_a_c, v_a_c, sink.reshape(A_KV_HEADS, A_GROUPS))
    o_b = _global_attention(q_b, jnp.concatenate([k_b, k_b_c], axis=1), jnp.concatenate([v_b, v_b_c], axis=1))
    return _merge_branches(o_a, o_b, proj[..., OFF_GA:], w_branch_a, w_branch_b, w_out)

def _context_token_mixer(h_c, kv_ctx, w_in, b_in, sink, q_norm_g, w_branch_a, w_branch_b, w_out):
    bsz, n_ctx, _ = h_c.shape
    k_a_c, v_a_c, k_b_c, v_b_c = kv_ctx
    q_a = (h_c @ w_in[:, OFF_QA:OFF_KA] + b_in[OFF_QA:OFF_KA]).reshape(bsz, n_ctx, A_KV_HEADS, A_GROUPS, HEAD_DIM)
    q_b = _qk_rms((h_c @ w_in[:, OFF_QB:OFF_KB] + b_in[OFF_QB:OFF_KB]).reshape(bsz, n_ctx, B_HEADS, HEAD_DIM),
                  q_norm_g).reshape(bsz, n_ctx, B_KV_HEADS, B_GROUPS, HEAD_DIM)
    gate_logits = h_c @ w_in[:, OFF_GA:] + b_in[OFF_GA:]
    o_a = _gqa_values(_sink_softmax(_gqa_scores(q_a, k_a_c), sink.reshape(A_KV_HEADS, A_GROUPS)), v_a_c)
    o_b = _gqa_values(jax.nn.softmax(_gqa_scores(q_b, k_b_c), axis=-1), v_b_c)
    return _merge_branches(o_a.reshape(bsz, n_ctx, -1), o_b.reshape(bsz, n_ctx, -1), gate_logits,
                           w_branch_a, w_branch_b, w_out)

def _conv_ffn(h, w_up, conv_w, conv_b, w_down):
    u = h @ w_up
    half = CONV_WIDTH // 2
    u = lax.conv_general_dilated(u, conv_w[:, None, :], window_strides=(1,), padding=((half, half),),
                                 dimension_numbers=("NWC", "WIO", "NWC"),
                                 feature_group_count=u.shape[-1]) + conv_b
    gate, val = jnp.split(u, 2, axis=-1)
    return (jax.nn.silu(gate) * val) @ w_down

def second_inputs(seed: int = 0) -> dict:
    key = jax.random.key(seed)
    ks = jax.random.split(key, 24)
    f32 = jnp.float32

    def normal(k, shape, scale):
        return jax.random.normal(k, shape, f32) * scale

    L = DEPTH
    return {
        "x": normal(ks[0], (BATCH, SEQ, D_MODEL), 1.0),
        "c": normal(ks[1], (BATCH, D_MODEL), 1.0),
        "ctx": normal(ks[2], (BATCH, CTX_LEN, D_MODEL), 1.0),
        "c_ctx": normal(ks[3], (D_MODEL,), 1.0),
        "w_mod": normal(ks[4], (L, D_MODEL, N_MOD * D_MODEL), 0.5 * D_MODEL ** -0.5),
        "b_mod": normal(ks[5], (L, N_MOD * D_MODEL), 0.02),
        "w_in": normal(ks[6], (L, D_MODEL, IN_COLS_2), D_MODEL ** -0.5),
        "b_in": normal(ks[7], (L, IN_COLS_2), 0.02),
        "attn_sink": normal(ks[8], (L, A_HEADS), 0.5),
        "q_norm_g": 1.0 + normal(ks[9], (L, HEAD_DIM), 0.05),
        "k_norm_g": 1.0 + normal(ks[10], (L, HEAD_DIM), 0.05),
        "w_branch_a": normal(ks[11], (L, A_HEADS * HEAD_DIM, D_MODEL), (A_HEADS * HEAD_DIM) ** -0.5),
        "w_branch_b": normal(ks[12], (L, B_HEADS * HEAD_DIM, D_MODEL), (B_HEADS * HEAD_DIM) ** -0.5),
        "w_out": normal(ks[13], (L, D_MODEL, D_MODEL), DEEPNORM_BETA * D_MODEL ** -0.5),
        "ln1_g": 1.0 + normal(ks[14], (L, D_MODEL), 0.05),
        "ln1_b": normal(ks[15], (L, D_MODEL), 0.02),
        "w_up": normal(ks[16], (L, D_MODEL, 2 * D_FF), D_MODEL ** -0.5),
        "conv_w": normal(ks[17], (L, CONV_WIDTH, 2 * D_FF), CONV_WIDTH ** -0.5),
        "conv_b": normal(ks[18], (L, 2 * D_FF), 0.02),
        "w_down": normal(ks[19], (L, D_FF, D_MODEL), DEEPNORM_BETA * D_FF ** -0.5),
        "ln2_g": 1.0 + normal(ks[20], (L, D_MODEL), 0.05),
        "ln2_b": normal(ks[21], (L, D_MODEL), 0.02),
    }

def second_block(x, c, ctx, c_ctx, w_mod, b_mod, w_in, b_in, attn_sink, q_norm_g, k_norm_g,
              w_branch_a, w_branch_b, w_out, ln1_g, ln1_b, w_up, conv_w, conv_b, w_down,
              ln2_g, ln2_b):
    n_tok = x.shape[1]
    rope = _axial_rope_tables(n_tok, x.dtype)
    for l in range(DEPTH):
        last = l == DEPTH - 1
        mod = jax.nn.silu(c) @ w_mod[l] + b_mod[l]
        shift1, scale1, gate1, shift2, scale2, gate2 = jnp.split(mod[:, None, :], N_MOD, axis=-1)
        n_mod_c = 2 if last else N_MOD
        mod_c = jax.nn.silu(c_ctx) @ w_mod[l, :, :n_mod_c * D_MODEL] + b_mod[l, :n_mod_c * D_MODEL]
        mods_c = jnp.split(mod_c, n_mod_c)
        h_c = ctx * (1.0 + mods_c[1]) + mods_c[0]
        kv_ctx = _context_kv(h_c, w_in[l], b_in[l], k_norm_g[l])

        h = x * (1.0 + scale1) + shift1
        y = _latent_token_mixer(h, kv_ctx, w_in[l], b_in[l], attn_sink[l], q_norm_g[l], k_norm_g[l],
                                w_branch_a[l], w_branch_b[l], w_out[l], rope)
        x = _layer_norm(DEEPNORM_ALPHA * x + gate1 * y, ln1_g[l], ln1_b[l])

        h = x * (1.0 + scale2) + shift2
        y = _conv_ffn(h, w_up[l], conv_w[l], conv_b[l], w_down[l])
        x = _layer_norm(DEEPNORM_ALPHA * x + gate2 * y, ln2_g[l], ln2_b[l])

        if not last:
            y_c = _context_token_mixer(h_c, kv_ctx, w_in[l], b_in[l], attn_sink[l], q_norm_g[l],
                                       w_branch_a[l], w_branch_b[l], w_out[l])
            ctx = _layer_norm(DEEPNORM_ALPHA * ctx + mods_c[2] * y_c, ln1_g[l], ln1_b[l])
            h_c = ctx * (1.0 + mods_c[4]) + mods_c[3]
            y_c = _conv_ffn(h_c, w_up[l], conv_w[l], conv_b[l], w_down[l])
            ctx = _layer_norm(DEEPNORM_ALPHA * ctx + mods_c[5] * y_c, ln2_g[l], ln2_b[l])
    return x


def setup_inputs(seed=0):
    out = dict(first_inputs(seed))
    for name, value in second_inputs(seed + 1).items():
        if name != "x":
            out[name + "_2"] = value
    return out


def reference(
    x, ffn1_norm, ffn1_w_gate, ffn1_w_up, ffn1_w_down, mix_norm, w_in, q_norm, k_norm, pool_w,
    pool_scale, w_out, ffn2_norm, ffn2_w_gate, ffn2_w_up, ffn2_w_down, c_2, ctx_2, c_ctx_2,
    w_mod_2, b_mod_2, w_in_2, b_in_2, attn_sink_2, q_norm_g_2, k_norm_g_2, w_branch_a_2,
    w_branch_b_2, w_out_2, ln1_g_2, ln1_b_2, w_up_2, conv_w_2, conv_b_2, w_down_2, ln2_g_2,
    ln2_b_2,
):
    x = first_block(
        x, ffn1_norm, ffn1_w_gate, ffn1_w_up, ffn1_w_down, mix_norm, w_in, q_norm, k_norm,
        pool_w, pool_scale, w_out, ffn2_norm, ffn2_w_gate, ffn2_w_up, ffn2_w_down,
    )
    return second_block(
        x, c_2, ctx_2, c_ctx_2, w_mod_2, b_mod_2, w_in_2, b_in_2, attn_sink_2, q_norm_g_2,
        k_norm_g_2, w_branch_a_2, w_branch_b_2, w_out_2, ln1_g_2, ln1_b_2, w_up_2, conv_w_2,
        conv_b_2, w_down_2, ln2_g_2, ln2_b_2,
    )


_drawn_inputs = setup_inputs


def setup_inputs(seed=0):
    import zlib

    import numpy as np

    out = dict(_drawn_inputs(seed))
    spreads = {}
    factors = {'ffn1_norm': 4.541,
     'mix_norm': 3.858,
     'q_norm': 8.0,
     'k_norm': 8.0,
     'ffn2_norm': 7.579,
     'ctx_2': 8.0,
     'c_ctx_2': 4.854,
     'b_mod_2': 6.121,
     'b_in_2': 8.0,
     'attn_sink_2': 8.0,
     'q_norm_g_2': 8.0,
     'k_norm_g_2': 8.0,
     'w_branch_a_2': 2.715,
     'w_branch_b_2': 3.194,
     'ln1_b_2': 2.873,
     'conv_b_2': 8.0,
     'ln2_b_2': 2.851}
    for name, (base, spread) in spreads.items():
        noise = np.random.default_rng([zlib.crc32(name.encode()), seed]).standard_normal(out[name].shape)
        drawn = base * np.exp(spread * noise) if base else spread * noise
        out[name] = jnp.asarray(drawn.astype(out[name].dtype))
    for name, factor in factors.items():
        out[name] = (out[name] * factor).astype(out[name].dtype)
    return out
```

```python
from contextlib import ExitStack

import numpy as np
import concourse.bass as bass
from concourse import mybir

F32 = mybir.dt.float32
F32R = mybir.dt.float32r
I32 = mybir.dt.int32
ALU = mybir.AluOpType
ACT = mybir.ActivationFunctionType
AX_X = mybir.AxisListType.X

P = 128
D = 1024
S = 512
KT = D // P
ST = S // P
FF = 2816
NF = FF // P
CTX = 256
CT = CTX // P
DH = 64
NH = 8
ATT = NH * DH
NKV = 2
IDX_HEADS, IDX_DIM, IDX_ROT = 4, 64, 32
IDX_COLS = IDX_HEADS * IDX_DIM + IDX_DIM + IDX_HEADS
TOPK = min(256, S // 4)
POOL_WINDOWS = (2, 4, 8, 16)
GRID_W = 64
THETA = 10000.0
RMS_EPS, QK_EPS, LN_EPS = 1e-6, 1e-6, 1e-5
IDX_SCALE = (IDX_HEADS ** -0.5) * (IDX_DIM ** -0.5)
ALPHA = 2.0 ** 0.25
NEG = -1e30
TAKEN = -3e38
RSQRT_MAGIC = float(0x5F3759DF)

PARTS = ((0, 8), (8, 8), (16, 6))
SLOTS = 4
SLAB = 8 * P

CONST = {}
_at = 0
for _name, _w in (("ident", P), ("causal", P), ("band", 640), ("band0", 512), ("inv_count", 16),
                  ("cos1", ST * DH), ("sin1", ST * DH), ("cosi", ST * IDX_ROT), ("sini", ST * IDX_ROT),
                  ("cos2", ST * DH), ("sin2", ST * DH)):
    CONST[_name] = (_at, _w)
    _at += _w
N_CONST = _at

VEC = {"ffn1_norm": (0, 0, 8), "mix_norm": (0, 8, 8), "ffn2_norm": (0, 16, 8), "b_mod": (0, 24, 48),
       "b_gate": (0, 72, 16), "ln1_g": (0, 88, 8), "ln1_b": (0, 96, 8), "ln2_g": (0, 104, 8),
       "ln2_b": (0, 112, 8), "c": (0, 120, 8), "c_ctx": (1, 0, 8), "pool_scale": (1, 8, 4),
       "conv_b": (1, 12, 44), "conv_w0": (2, 0, 44), "conv_w1": (2, 44, 44), "conv_w2": (3, 0, 44)}


def constants():
    out = np.zeros((P, N_CONST), np.float32)
    row, col = np.arange(P)[:, None], np.arange(P)[None, :]

    def put(name, value):
        a, w = CONST[name]
        out[:, a:a + w] = value.reshape(P, w)

    neg = np.float32(NEG)
    put("ident", (row == col).astype(np.float32))
    put("causal", np.where(col > row, neg, np.float32(0)))
    before = np.where(col >= row, np.float32(0), neg)
    after = np.where(col <= row, np.float32(0), neg)
    zero = np.zeros((P, P), np.float32)
    put("band", np.concatenate([zero, zero, before, zero, after], axis=1))
    put("band0", np.concatenate([zero, zero, zero, after], axis=1))
    put("inv_count", np.broadcast_to(1 / (np.arange(16, dtype=np.float32) + 1), (P, 16)))
    pos = np.arange(S, dtype=np.float32).reshape(ST, P).T

    def table(parts):
        cos, sin = [], []
        for where, half in parts:
            inv = np.float32(THETA) ** (-np.arange(half, dtype=np.float32) / np.float32(half))
            ang = (where[:, :, None] * inv).astype(np.float32)
            cos += [np.cos(ang), np.cos(ang)]
            sin += [-np.sin(ang), np.sin(ang)]
        return np.concatenate(cos, axis=2), np.concatenate(sin, axis=2)

    for name, parts in (("1", [(pos, DH // 2)]), ("i", [(pos, IDX_ROT // 2)]),
                        ("2", [(pos // GRID_W, DH // 4), (pos % GRID_W, DH // 4)])):
        cos, sin = table(parts)
        put("cos" + name, cos)
        put("sin" + name, sin)
    return out


class Chain:

    def __init__(self, engine, sem):
        self.engine, self.sem, self.n, self.links = engine, sem, 0, 0

    def link(self, instruction):
        instruction.then_inc(self.sem, 1)
        self.n, self.links = self.n + 1, self.links + 1
        self.engine.wait_ge(self.sem, self.n)

    def loop(self, first, end, per, body):
        if first >= end:
            return
        start, links = self.n, self.links
        if end - first == 1:
            body(first)
        else:
            with self.engine.Fori(first, end) as i:
                self.n = start + (i - first) * per
                body(i)
        assert self.links - links == per, (self.links - links, per)
        self.n = start + (end - first) * per


def loop(engine, first, end, body):
    if end - first == 1:
        body(first)
    elif end > first:
        with engine.Fori(first, end) as i:
            body(i)


def build(nc, t):
    stack = ExitStack()
    with stack:
        _build(nc, t, stack)


def _build(nc, t, stack):
    stages = []

    def stage(name, slabs, width, sources):
        base = sum(s["slabs"] for s in stages)
        dmas = len(sources(0, 0))
        raw = sum(s["slabs"] // SLOTS * s["dmas"] for s in stages)
        stages.append(dict(name=name, slabs=slabs, width=width, sources=sources, base=base,
                           dmas=dmas, raw=raw, its=slabs // SLOTS))

    def kview(w):
        return w.rearrange("(k p) n -> p k n", p=P)

    def ffn(name, gate, up, up_off, down):
        for n, (f0, nf) in enumerate(PARTS):
            stage(f"{name}_up{n}", 2 * nf, SLAB, lambda i, j, f0=f0: [
                (0, kview(gate if j % 2 == 0 else up)[:, :, bass.ds(
                    (i * 2 + (f0 + j // 2)) * P + (up_off if j % 2 else 0), P)])])
            stage(f"{name}_down{n}", KT, nf * P, lambda i, j, f0=f0, nf=nf: [
                (0, kview(down[f0 * P:(f0 + nf) * P, :])[:, :, bass.ds((i * 4 + j) * P, P)])])

    def columns(name, w, first, n):
        stage(name, n, SLAB, lambda i, j: [(0, kview(w)[:, :, bass.ds((i * 4 + j) * P + first, P)])])

    def rows(name, w, first, width, per):
        stage(name, KT // per, per * width, lambda i, j: [
            (0, kview(w)[:, j * per:(j + 1) * per, first:first + width])])

    w_in, w_in2 = t["w_in"][0], t["w_in_2"][0]
    ffn("f1", t["ffn1_w_gate"][0], t["ffn1_w_up"][0], 0, t["ffn1_w_down"][0])
    stage("ctxkv", 4, SLAB, lambda i, j: [(0, kview(w_in2)[:, 4 * (j % 2):4 * (j % 2) + 4,
                                               (512, 1280)[j // 2]:(512, 1280)[j // 2] + 256])])
    rows("idx", w_in, 3 * ATT, IDX_COLS, 2)
    columns("pool", w_in, 3 * ATT + IDX_COLS, 4)
    rows("q", w_in, 0, ATT, 2)
    rows("k", w_in, ATT, ATT, 2)
    rows("v", w_in, 2 * ATT, ATT, 2)
    columns("out1", t["w_out"][0], 0, KT)
    ffn("f2", t["ffn2_w_gate"][0], t["ffn2_w_up"][0], 0, t["ffn2_w_down"][0])
    for g in range(3):
        rows(f"proj{g}", w_in2, 512 * g, 512, 2)
    columns("gates", w_in2, 1536, 16)
    wa, wb = t["w_branch_a_2"][0], t["w_branch_b_2"][0]
    stage("merge", KT, SLAB, lambda i, j: [(0, kview(wa)[:, :, bass.ds((i * 4 + j) * P, P)]),
                                           (4, kview(wb)[:, :, bass.ds((i * 4 + j) * P, P)])])
    columns("out2", t["w_out_2"][0], 0, KT)
    ffn("f3", t["w_up_2"][0], t["w_up_2"][0], FF, t["w_down_2"][0])
    stage_of = {s["name"]: s for s in stages}
    nxt = {a["name"]: b for a, b in zip(stages, stages[1:])}

    by_act = {"idx", "pool", "q", "k", "v", "gates"}
    drain_base, totals = {}, {"v": KT, "a": 0}
    for s in stages:
        who = "a" if s["name"] in by_act else "v"
        drain_base[s["name"]] = totals[who]
        totals[who] += s["slabs"]

    def sb(name, cols, dt=F32):
        return stack.enter_context(nc.sbuf_tensor(name, [P, cols], dt))

    first_byte = {}

    def region(name, cols):
        first_byte[name] = (nc.sbuf_base, cols * 4)
        return stack.enter_context(nc.sbuf_tensor(name + "_room", [P, cols], F32))

    def at(name, where, cols, dt=F32):
        room, first = where
        base, size = first_byte[room]
        assert (first + cols) * 4 <= size, (name, room)
        return nc.alloc_sbuf_tensor_at(name, [P, cols], dt, offset=base + first * 4)

    x = sb("x", KT * S)
    region("act", 2 * KT * S)
    region("hid", 2 * KT * S)
    region("free", 8320)
    region("kv", 4608)
    actH = at("actH", ("act", 0), KT * S, F32R)
    actL = at("actL", ("act", KT * S), KT * S, F32R)
    hidH = at("hidH", ("hid", 0), KT * S, F32R)
    hidL = at("hidL", ("hid", KT * S), KT * S, F32R)
    raw = sb("raw", SLOTS * SLAB)
    wH = sb("wH", SLOTS * SLAB, F32R)
    wL = sb("wL", SLOTS * SLAB, F32R)
    const = sb("const", N_CONST)
    cols = sb("cols", 4 * P)
    ones = sb("ones", P)
    one = sb("one", 1)
    zero = sb("zero", 1)
    rB = sb("rB", S)
    acc = sb("acc", S)
    sq = sb("sq", S)
    rn = sb("rn", ST)
    small = sb("small", 4 * 64)
    modc = sb("modc", 48)
    modx = sb("modx", 16)
    silu_c = sb("silu_c", 16)
    gain1 = sb("gain1", 2 * DH)
    gain2 = sb("gain2", 2 * DH)
    ropeT = sb("ropeT", 4 * ST * DH)
    sink = sb("sink", 2 * NH)
    biasx = sb("biasx", 512)
    kTA = at("kTA", ("kv", 0), NKV * (CTX + S))
    kTB = at("kTB", ("kv", 1536), NKV * (CTX + S))
    vA = at("vA", ("kv", 3072), (CT + ST) * NKV * DH)
    vB = at("vB", ("kv", 3840), (CT + ST) * NKV * DH)
    pool_head = sb("pool_head", 16)
    inv_w = sb("inv_w", len(POOL_WINDOWS))
    k_scale = sb("k_scale", ST * NH)
    ssq = sb("ssq", 64)
    stat = sb("stat", 4 * 32)
    ln_col = sb("ln_col", 2 * KT)

    def cv(name):
        a, w = CONST[name]
        return const[:, a:a + w]

    ident = cv("ident")

    def col(name, n):
        g, first, _ = VEC[name]
        return cols[:, bass.ds(n + (g * P + first), 1)]

    g1 = at("g1", ("free", 0), S)
    sg = at("sg", ("free", S), S)
    ur = at("ur", ("free", 2 * S), S)
    h = at("h", ("free", 3 * S), S)
    xnat = at("xnat", ("hid", 0), ST * D)
    vec_rows = at("vec_rows", ("hid", ST * D), 4 * P)
    mod_raw = at("mod_raw", ("free", 4 * S), 4096)
    mod_acc = at("mod_acc", ("free", 4 * S + 4096), 1024)
    hcH = at("hcH", ("free", 4 * S), KT * CTX, F32R)
    hcL = at("hcL", ("free", 4 * S + KT * CTX), KT * CTX, F32R)
    ctx_nat = at("ctx_nat", ("kv", 0), CT * D)
    tA = at("tA", ("free", 0), S)
    tB = at("tB", ("free", S), S)
    u_pool = at("u_pool", ("free", 2 * S), 4 * S)
    work = at("work", ("free", 6 * S), 9 * P)
    v1 = at("v1", ("free", 6 * S + 9 * P), ST * ATT)
    pool_w = at("pool_w", ("free", 10 * S + 9 * P), 4 * P)
    kctx = at("kctx", ("free", 11 * S + 9 * P), 4 * P)
    rel = at("rel", ("free", 12 * S + 9 * P), 2 * S)
    qiT = at("qiT", ("hid", 0), 2 * S)
    kiT = at("kiT", ("hid", 2 * S), S)
    pi = at("pi", ("hid", KT * S), ST * IDX_COLS)
    q1 = at("q1", ("hid", 0), ST * ATT)
    k1 = at("k1", ("hid", KT * S), ST * ATT)
    qT1 = at("qT1", ("act", 0), 4 * S)
    kT1 = at("kT1", ("act", 4 * S), 4 * S)
    attn1 = at("attn1", ("free", 2 * S), ST * ATT)
    prob = at("prob", ("act", 8 * S), 3 * 768)
    probT = at("probT", ("act", 8 * S + 3 * 768), 2 * 768)
    nat = at("nat", ("free", 0), ST * 1536)
    bias2 = at("bias2", ("free", ST * 1536), 1536)
    tC = at("tC", ("free", ST * 1536 + 1536), 640)
    gates = at("gates", ("hid", 0), 16 * S)
    qTA = at("qTA", ("act", 0), 4 * S)
    qTB = at("qTB", ("act", 4 * S), 4 * S)
    attnA = at("attnA", ("free", 0), ST * ATT)
    attnB = at("attnB", ("free", ST * ATT), ST * ATT)
    mA = at("mA", ("free", 2 * ST * ATT), S)
    mB = at("mB", ("free", 2 * ST * ATT + S), S)
    cg = at("cg", ("free", 0), 2 * S)
    cu = at("cu", ("free", 2 * S), 2 * S)
    h3 = at("h3", ("free", 6 * S), S)
    sq2 = at("sq2", ("free", 4 * S), 2 * S)
    out_nat = at("out_nat", ("free", 8 * S), ST * D)

    ps = stack.enter_context(nc.psum_tensor("ps", [P, 8, 512], F32))

    def sem(name):
        return stack.enter_context(nc.semaphore(name))

    x_in = [sem(f"x_in{q}") for q in range(ST)]
    vec_in, const_in, misc_in, ctx_in, bias_in = sem("vec_in"), sem("const_in"), sem("misc_in"), sem("ctx_in"), sem("bias_in")
    raw_in = [sem(f"raw_in{j}") for j in range(SLOTS)]
    mod_in = [sem(f"mod_in{q}") for q in range(2)]
    cleared = sem("cleared")
    hi_ready = sem("hi_ready")
    lo_ready = sem("lo_ready")
    slab_done = sem("slab_done")
    drained_v, drained_a = sem("drained_v"), sem("drained_a")
    v_step, a_step, p_step = sem("v_step"), sem("a_step"), sem("p_step")
    vec_T, cols_ready = sem("vec_T"), sem("cols_ready")
    xT = sem("xT")
    act_hi = sem("act_hi")
    act_ready = sem("act_ready")
    hid_ready = sem("hid_ready")
    sq_ready = sem("sq_ready")
    acc_done = sem("acc_done")
    row_sum, rn_ready, row_bcast = sem("row_sum"), sem("rn_ready"), sem("row_bcast")
    stat_out = sem("stat_out")
    silu_ready = sem("silu_ready")
    silu_c_ready = sem("silu_c_ready")
    mod_half, mod_sum, mod_cols = sem("mod_half"), sem("mod_sum"), sem("mod_cols")
    ctx_T, ctx_drained, hc_ready = sem("ctx_T"), sem("ctx_drained"), sem("hc_ready")
    kctx_ready, kctx_T, kctx_out = sem("kctx_ready"), sem("kctx_T"), sem("kctx_out")
    idx_rot, idx_T, idx_cols, idx_qk, idx_rel, idx_rel_used = (sem(n) for n in (
        "idx_rot", "idx_T", "idx_cols", "idx_qk", "idx_rel", "idx_rel_used"))
    scored = sem("scored")
    pooled, pool_mm, pool_hi, pool_lo = sem("pooled"), sem("pool_mm"), sem("pool_hi"), sem("pool_lo")
    k_scaled, k_rot = sem("k_scaled"), sem("k_rot")
    qk_sq, qk_rot, qk_T, qk_out = sem("qk_sq"), sem("qk_rot"), sem("qk_T"), sem("qk_out")
    att_qk, q2_rot, q2_T, q2_out, k2_out = (sem(n) for n in ("att_qk", "q2_rot", "q2_T", "q2_out", "k2_out"))
    logit, shifted, probs, prob_T, probT_a, probT_v, pv, attn_out = (sem(n) for n in (
        "logit", "shifted", "probs", "prob_T", "probT_a", "probT_v", "pv", "attn_out"))
    at_T, at_hi, at_lo = sem("at_T"), sem("at_hi"), sem("at_lo")
    gate_ready = sem("gate_ready")
    mean_sum, centred, scaled = sem("mean_sum"), sem("centred"), sem("scaled")
    conv_c, conv_act = sem("conv_c"), sem("conv_act")
    fin_ready, fin_T, fin_out, stored = sem("fin_ready"), sem("fin_T"), sem("fin_out"), sem("stored")

    def units1():
        for tile in reversed(range(ST)):
            for head in range(NH):
                w, off = P * (tile + 1), DH * (head % 2)
                yield dict(W=w, qT=qT1[off:off + DH, (head // 2) * S + tile * P:][:, 0:P],
                           keys=[(kT1[off:off + DH, (head // 2) * S:(head // 2) * S + w], 0)],
                           mask=cv("causal") if tile == 0 else work[:, P * (tile * (tile + 1) // 2 - 1):][:, 0:w],
                           v=[v1[:, b * ATT + head * DH:][:, 0:DH] for b in range(tile + 1)],
                           out=attn1[:, tile * ATT + head * DH:][:, 0:DH], sink=None)

    def units2(qT, kT, v, out, banded):
        for tile in range(ST):
            for head in range(NH):
                kv, off = head // (NH // NKV), DH * (head % 2)
                first = max(tile - 1, 0) if banded else 0
                last = min(tile + 1, ST - 1) if banded else ST - 1
                key0 = kv * (CTX + S)
                w = CTX + P * (last - first + 1)
                runs, at_col = [], 0
                for a, b in ((0, CTX), (CTX + first * P, CTX + (last + 1) * P)):
                    while a < b:
                        n = min(b - a, 512 - at_col % 512)
                        if runs and runs[-1][1] == a and at_col % 512:
                            runs[-1] = (runs[-1][0], a + n, runs[-1][2])
                        else:
                            runs.append((a, a + n, at_col))
                        a, at_col = a + n, at_col + n
                mask = zero[:, 0:1].broadcast_to([P, w])
                if banded:
                    mask = cv("band0") if tile == 0 else cv("band")[:, 0:w]
                yield dict(W=w, qT=qT[off:off + DH, (head // 2) * S + tile * P:][:, 0:P],
                           keys=[(kT[off:off + DH, key0 + a:key0 + b], c) for a, b, c in runs],
                           mask=mask,
                           v=[v[:, b * NKV * DH + kv * DH:][:, 0:DH]
                              for b in [*range(CT), *range(CT + first, CT + last + 1)]],
                           out=out[:, tile * ATT + head * DH:][:, 0:DH], sink=head if banded else None)

    group1 = list(units1())
    group2 = list(units2(qTA, kTA, vA, attnA, True)) + list(units2(qTB, kTB, vB, attnB, False))


    ACC_TOTAL = [KT, 2 * KT, 3 * KT, 5 * KT, 7 * KT]
    ACT_BEFORE = {"f1": 0, "f2": 2 * KT, "f3": 5 * KT}
    SILU_BEFORE = {f"f{a}_up{n}": NF * (a - 1) + f0 for a in (1, 2) for n, (f0, _) in enumerate(PARTS)}
    MISC_DMAS = 7
    wide = [u["W"] > 512 for u in group1 + group2]
    WIDE = [sum(wide[:n]) for n in range(len(wide) + 1)]
    vec_sources = [("ffn1_norm", t["ffn1_norm"][0]), ("mix_norm", t["mix_norm"][0]), ("ffn2_norm", t["ffn2_norm"][0]),
                   ("b_mod", t["b_mod_2"][0]), ("b_gate", t["b_in_2"][0, 1536:]), ("ln1_g", t["ln1_g_2"][0]),
                   ("ln1_b", t["ln1_b_2"][0]), ("ln2_g", t["ln2_g_2"][0]), ("ln2_b", t["ln2_b_2"][0]),
                   ("c", t["c_2"][0]), ("c_ctx", t["c_ctx_2"]), ("pool_scale", t["pool_scale"][0]),
                   ("conv_b", t["conv_b_2"][0]), ("conv_w0", t["conv_w_2"][0, 0]), ("conv_w1", t["conv_w_2"][0, 1]),
                   ("conv_w2", t["conv_w_2"][0, 2])]
    VEC_DMAS = len(vec_sources)

    def tile(buf, n, w=S):
        return buf[:, bass.ds(n * w, w)]

    def bank(b, w=512, first=0):
        return ps[:, b, first:first + w]

    block = stack.enter_context(nc.Block())

    def rotate(E, link, v, tmp, heads, groups, half, cos, sin, last=None):
        w = groups * 2 * half
        x5 = v if groups == 1 else v.rearrange("p h (g r) -> p h g r", g=groups)
        t5 = tmp if groups == 1 else tmp.rearrange("p h (g r) -> p h g r", g=groups)
        s5 = sin if groups == 1 else sin.rearrange("p (g r) -> p g r", g=groups)
        for to, frm in ((0, half), (half, 0)):
            if groups == 1:
                link(E.tensor_tensor(t5[:, :, to:to + half], x5[:, :, frm:frm + half],
                                     s5[:, to:to + half].unsqueeze(1).broadcast_to([P, heads, half]), ALU.mult))
            else:
                link(E.tensor_tensor(t5[:, :, :, to:to + half], x5[:, :, :, frm:frm + half],
                                     s5[:, :, to:to + half].unsqueeze(1).broadcast_to([P, heads, groups, half]),
                                     ALU.mult))
        link(E.tensor_tensor(v, v, cos.unsqueeze(1).broadcast_to([P, heads, w]), ALU.mult))
        ins = E.tensor_tensor(v, v, tmp, ALU.add)
        if last is None:
            link(ins)
        else:
            ins.then_inc(last, 1)

    def gained(n, part, q):
        return ropeT[:, (2 * n + part) * ST * DH + q * DH:][:, 0:DH]

    def heads_rotated(E, chain, src, n, tmp, scales, done):
        link = chain.link
        for q in range(ST):
            v = src[:, q * ATT:(q + 1) * ATT].rearrange("p (h d) -> p h d", h=NH)
            link(E.tensor_tensor(v, v, scales[:, q * NH:][:, 0:NH].unsqueeze(2).broadcast_to([P, NH, DH]), ALU.mult))
            rotate(E, link, v, tmp[:].rearrange("p (h d) -> p h d", h=NH), NH, 1, DH // 2,
                   gained(n, 0, q), gained(n, 1, q), last=done)
            chain.engine.wait_ge(done, q + 1)

    @block.sync
    def _(sp):
        for q in range(ST):
            sp.dma_start(xnat[:, q * D:(q + 1) * D], t["x"][0, q * P:(q + 1) * P, :]).then_inc(x_in[q], 16)

        def slab(st, i, j, first=False):
            if not first:
                sp.wait_ge(lo_ready, i * 4 + (st["base"] + j - 3))
            for c, src in st["sources"](i, j):
                k, n = src.shape[1], src.shape[2]
                dst = raw[:, j * SLAB + c * P:j * SLAB + c * P + k * n].rearrange("p (k n) -> p k n", k=k)
                sp.dma_start(dst, src).then_inc(raw_in[j], 16)

        def slabs(st, first, end):
            def body(i):
                for j in range(SLOTS):
                    slab(st, i, j)
            loop(sp, first, end, body)

        for st in stages:
            begun = 0
            if st["name"] == "f1_up0":
                for j in range(SLOTS):
                    slab(st, 0, j, first=True)
                begun = 1
            if st["name"] == "k":
                sp.wait_ge(mod_cols, 12)
                sp.wait_ge(slab_done, stage_of["idx"]["base"])
                sp.dma_start(pool_w[:].rearrange("c (g d) -> c g d", g=4),
                             t["pool_w"][0].rearrange("g c d -> c g d")).then_inc(misc_in, 16)
            if st["name"] == "f2_up1":
                sp.wait_ge(slab_done, stage_of["f2_up0"]["base"])
                sp.dma_start(bias2[:], t["b_in_2"][0:1, 0:1536].broadcast_to([P, 1536])).then_inc(bias_in, 16)
            slabs(st, begun, st["its"])
        for n in range(2 * ST):
            half, q = n // ST, n % ST
            sp.wait_ge(fin_out, n + 1)
            sp.dma_start(t["out"][0, q * P:(q + 1) * P, half * 512:(half + 1) * 512],
                         out_nat[:, q * D + half * 512:q * D + half * 512 + 512]).then_inc(stored, 16)
        sp.wait_ge(stored, 16 * 2 * ST)

    @block.gpsimd
    def _(pool):
        nc.gpsimd.memset(vec_rows[:], 0.0).then_inc(cleared, 1)
        nc.gpsimd.memset(ones[:], 1.0 / D).then_inc(cleared, 1)
        nc.gpsimd.memset(one[:], 1.0).then_inc(cleared, 1)
        nc.gpsimd.memset(zero[:], 0.0).then_inc(cleared, 1)
        for g, w in enumerate(POOL_WINDOWS):
            nc.gpsimd.memset(inv_w[:, g:g + 1], 1.0 / w).then_inc(cleared, 1)

        def lows(st, i, then=None):
            for j in range(SLOTS):
                a, w = j * SLAB, st["width"]
                pool.wait_ge(hi_ready, i * 4 + (st["base"] + j + 1))
                nc.gpsimd.tensor_tensor(wL[:, a:a + w], raw[:, a:a + w], wH[:, a:a + w].bitcast(F32),
                                        ALU.subtract).then_inc(lo_ready, 1)
                if then:
                    then(j)

        chain = Chain(pool, p_step)
        link = chain.link
        G = nc.gpsimd

        def pooling(g):
            u, w = tile(u_pool, g), POOL_WINDOWS[g]
            pool.wait_ge(drained_a, drain_base["pool"] + g + 1)
            pool.wait_ge(stat_out, 2)
            link(G.tensor_tensor(u, u, rB[:], ALU.mult))
            src, step, bufs = u, 1, [tB, sq]
            while step < w:
                dst = bufs[0][:]
                bufs = bufs[::-1]
                G.tensor_tensor(dst[:, step:], src[:, step:], src[:, 0:S - step], ALU.add)
                link(G.tensor_copy(dst[:, 0:step], src[:, 0:step]))
                src, step = dst, 2 * step
            head = pool_head[:, 0:w - 1]
            link(G.tensor_tensor(head, src[:, 0:w - 1], cv("inv_count")[:, 0:w - 1], ALU.mult))
            link(G.tensor_tensor(head, head, u[:, 0:w - 1], ALU.subtract))
            link(G.tensor_tensor(src, src, inv_w[:, g:g + 1].broadcast_to([P, S]), ALU.mult))
            link(G.tensor_tensor(u, src, u, ALU.subtract))
            G.tensor_copy(u[:, 0:w - 1], head).then_inc(pooled, 1)
            pool.wait_ge(pooled, g + 1)

        for st in stages:
            if st["name"] == "q":
                lows(st, 0, then=pooling)
            elif st["name"] == "out1":
                pool.wait_ge(k_scaled, 1)
                heads_rotated(G, chain, k1, 1, sq, k_scale[:], k_rot)
                loop(pool, 0, st["its"], lambda i, st=st: lows(st, i))
            else:
                loop(pool, 0, st["its"], lambda i, st=st: lows(st, i))

    @block.tensor
    def _(pe):
        def product(out, a, b, first, last):
            return nc.tensor.matmul(out, a, b, start=first, stop=last)

        def split_product(out, wh, wl, xh, xl, first, last):
            product(out, wh, xh, first, False)
            product(out, wh, xl, False, False)
            return product(out, wl, xh, False, last)

        def row_sums(n):
            pe.wait_ge(acc_done, ACC_TOTAL[n])
            for q in range(ST):
                mm = product(ps[:, 4, q:q + 1], acc[:, q * P:(q + 1) * P], ones[:, 0:1], True, True)
            mm.then_inc(row_sum, 1)

        def spread_rows(n):
            pe.wait_ge(rn_ready, n + 1)
            for q in range(ST):
                mm = product(bank(5, P, q * P), rn[:, q:q + 1].broadcast_to([P, P]), ident, True, True)
            mm.then_inc(row_bcast, 1)

        def feature_tiles(name, opH, opL, ready, K=KT, drained=drained_v, after=None, finish=None, peel=0):
            st = stage_of[name]

            def body(i):
                for j in range(SLOTS):
                    pe.wait_ge(lo_ready, i * 4 + (st["base"] + j + 1))
                    pe.wait_ge(drained, i * 4 + (drain_base[name] + j - 3))
                    for k in range(K):
                        if j == 0:
                            pe.wait_ge(ready[0], ready[1] + k + 1)
                        a = j * SLAB + k * P
                        mm = split_product(bank(j), wH[:, a:a + P], wL[:, a:a + P],
                                           opH[:, k * S:(k + 1) * S], opL[:, k * S:(k + 1) * S], k == 0, k == K - 1)
                    mm.then_inc(slab_done, 1)
                    if after and isinstance(i, int):
                        after(j)
                if finish:
                    finish(i)
            for i in range(peel):
                body(i)
            loop(pe, peel, st["its"], body)

        def token_tiles(name, width, bank0, before, after=None):
            st = stage_of[name]
            before()
            for j in range(SLOTS):
                pe.wait_ge(lo_ready, st["base"] + j + 1)
                for kk in range(2):
                    k, a = 2 * j + kk, j * SLAB + kk * width
                    for q in range(ST):
                        xh, xl = (b[:, k * S + q * P:k * S + (q + 1) * P] for b in (actH, actL))
                        o = bank(bank0 + q, width)
                        product(o, xh, wH[:, a:a + width], k == 0, False)
                        product(o, xl, wH[:, a:a + width], False, False)
                        mm = product(o, xh, wL[:, a:a + width], False, k == KT - 1)
                mm.then_inc(slab_done, 1)
                if after:
                    after(j)

        pe.wait_ge(const_in, 16)
        pe.wait_ge(vec_in, VEC_DMAS * 16)
        for g in range(4):
            mm = nc.tensor.transpose(bank(7, P, g * P), vec_rows[:, g * P:(g + 1) * P], ident)
        mm.then_inc(vec_T, 1)
        for k in range(KT):
            if k >= 4:
                pe.wait_ge(drained_v, k - 3)
            for q in range(ST):
                if k == 0:
                    pe.wait_ge(x_in[q], 16)
                mm = nc.tensor.transpose(bank(k % 4, P, q * P), xnat[:, q * D + k * P:q * D + (k + 1) * P], ident)
            mm.then_inc(xT, 1)

        def up_down(name, hid0, first_hook, finish=None):
            for n, (f0, nf) in enumerate(PARTS):
                hooked = first_hook if n == 0 else None
                feature_tiles(f"{name}_up{n}", actH, actL, (act_ready, ACT_BEFORE[name]), after=hooked,
                              peel=1 if n == 0 else 0,
                              finish=(lambda i, n=n: finish(n, i)) if finish else None)
                if name == "f1" and n == 2:
                    context_turn()
                feature_tiles(f"{name}_down{n}", hidH, hidL, (hid_ready, hid0 + f0), K=nf)

        def norm_hook(n):
            def after(j):
                if j == 0:
                    row_sums(n)
                if j == 1:
                    spread_rows(n)
            return after

        def mod_sums(i, ctx_too):
            pe.wait_ge(mod_half, (i + 1) * 2)
            if not isinstance(i, int) or i > 0:
                pe.wait_ge(mod_cols, i)
            for q in range(8 if ctx_too else 4):
                mm = product(ps[:, 6, q:q + 1], mod_acc[:, q * P:(q + 1) * P], one[:, 0:1], True, True)
            mm.then_inc(mod_sum, 1)

        def context_turn():
            pe.wait_ge(ctx_in, 16)
            for k in range(KT):
                if k < 4:
                    pe.wait_ge(mod_cols, 11)
                    pe.wait_ge(stat_out, 1)
                    pe.wait_ge(cols_ready, 1)
                else:
                    pe.wait_ge(ctx_drained, k - 3)
                for q in range(CT):
                    mm = nc.tensor.transpose(bank(4 + k % 4, P, q * P),
                                             ctx_nat[:, q * D + k * P:q * D + (k + 1) * P], ident)
                mm.then_inc(ctx_T, 1)

        def f1_finish(n, i):
            chunk = i + n * 4
            mod_sums(chunk, n == 0)

        up_down("f1", 0, norm_hook(0), f1_finish)
        pe.wait_ge(ctx_drained, KT)
        mod_sums(11, False)

        st = stage_of["ctxkv"]
        for j in range(SLOTS):
            pe.wait_ge(lo_ready, st["base"] + j + 1)
            for kk in range(4):
                k, a = 4 * (j % 2) + kk, j * SLAB + kk * 256
                pe.wait_ge(hc_ready, k + 1)
                for q in range(CT):
                    b = 2 * (j // 2) + q
                    if k == 0:
                        pe.wait_ge(drained_v, drain_base["ctxkv"] - 3 + b)
                    xh, xl = (c[:, k * CTX + q * P:k * CTX + (q + 1) * P] for c in (hcH, hcL))
                    product(bank(b, 256), xh, wH[:, a:a + 256], k == 0, False)
                    product(bank(b, 256), xl, wH[:, a:a + 256], False, False)
                    mm = product(bank(b, 256), xh, wL[:, a:a + 256], False, k == KT - 1)
            mm.then_inc(slab_done, 1)
            if j == 0:
                row_sums(1)
            if j == 2:
                spread_rows(1)

        def before_idx():
            pe.wait_ge(act_ready, 2 * KT)
            pe.wait_ge(stat_out, 2)
            pe.wait_ge(mod_cols, 12)

        token_tiles("idx", IDX_COLS, 4, before_idx)

        def idx_turns():
            pe.wait_ge(idx_rot, ST)
            for q in range(ST):
                a = q * IDX_COLS
                for pair in range(2):
                    nc.tensor.transpose(bank(4 + pair, P, q * P), pi[:, a + pair * P:a + (pair + 1) * P], ident)
                mm = nc.tensor.transpose(ps[0:IDX_DIM, 6, q * P:(q + 1) * P], pi[:, a + 2 * P:a + 2 * P + IDX_DIM], ident)
            mm.then_inc(idx_T, 1)

        def idx_scores():
            pe.wait_ge(idx_cols, 4)
            for n in range((ST - 1) * IDX_HEADS):
                q, head = n // IDX_HEADS + 1, n % IDX_HEADS
                off = IDX_DIM * (head % 2)
                if n >= 4:
                    pe.wait_ge(idx_rel, n - 3)
                product(bank(4 + n % 4, P * (q + 1)), qiT[off:off + IDX_DIM, (head // 2) * S + q * P:][:, 0:P],
                        kiT[off:off + IDX_DIM, 0:P * (q + 1)], True, True).then_inc(idx_qk, 1)

        st = stage_of["pool"]
        for j in range(SLOTS):
            pe.wait_ge(lo_ready, st["base"] + j + 1)
            pe.wait_ge(drained_v, drain_base["ctxkv"] + j + 1)
            for k in range(KT):
                a = j * SLAB + k * P
                mm = split_product(bank(j), wH[:, a:a + P], wL[:, a:a + P], actH[:, k * S:(k + 1) * S],
                                   actL[:, k * S:(k + 1) * S], k == 0, k == KT - 1)
            mm.then_inc(slab_done, 1)
            if j == 1:
                idx_turns()
        idx_scores()
        token_tiles("q", ATT, 4, lambda: pe.wait_ge(idx_rel, 12))
        token_tiles("k", ATT, 0, lambda: pe.wait_ge(drained_a, drain_base["pool"] + 4))
        token_tiles("v", ATT, 4, lambda: pe.wait_ge(drained_a, drain_base["q"] + 4))

        pe.wait_ge(drained_a, drain_base["k"] + 4)
        pe.wait_ge(kctx_ready, 2)
        for n in range(4):
            mm = nc.tensor.transpose(bank(0, P, n * P), kctx[:, n * P:(n + 1) * P], ident)
        mm.then_inc(kctx_T, 1)
        pe.wait_ge(pooled, 4)
        pe.wait_ge(misc_in, MISC_DMAS * 16 + 16)
        pe.wait_ge(drained_a, drain_base["v"] + 4)
        for g in range(4):
            product(bank(4 + g), pool_w[:, g * P:(g + 1) * P], u_pool[:, g * S:(g + 1) * S], True, True).then_inc(pool_mm, 1)
        for n in range(2 * ST):
            src, q = (q1, k1)[n // ST], n % ST
            pe.wait_ge((qk_rot, k_rot)[n // ST], q + 1)
            if n == 0:
                pe.wait_ge(kctx_out, 8)
            if n >= 4:
                pe.wait_ge(qk_out, n - 3)
            for pair in range(4):
                mm = nc.tensor.transpose(bank(n % 4, P, pair * P), src[:, q * ATT + pair * P:][:, 0:P], ident)
            mm.then_inc(qk_T, 1)

        def warm(n):
            for _ in range(n):
                product(bank(5), ident, cv("band")[:, 0:512], True, True)

        def attention(units, n0):
            def logits(n):
                u = units[n - n0]
                if n - n0 >= 2:
                    pe.wait_ge(logit, n - 1)
                b = 2 * (n % 2)
                for keys, c in u["keys"]:
                    w = keys.shape[1]
                    mm = product(bank(b + c // 512, w, c % 512), u["qT"], keys, True, True)
                mm.then_inc(att_qk, 1)

            def turn(n):
                u = units[n - n0]
                pe.wait_ge(probs, n + 1)
                if n > 0:
                    pe.wait_ge(probT_a, n)
                if n > n0 and units[n - 1 - n0]["W"] > 512:
                    pe.wait_ge(probT_v, WIDE[n])
                for b in range(u["W"] // P):
                    mm = nc.tensor.transpose(bank(4 + b // 4, P, (b % 4) * P),
                                             prob[:, (n % 3) * 768 + b * P:][:, 0:P], ident)
                mm.then_inc(prob_T, 1)

            def values(n):
                u = units[n - n0]
                pe.wait_ge(probT_a, n + 1)
                if u["W"] > 512:
                    pe.wait_ge(probT_v, WIDE[n + 1])
                if n >= 2:
                    pe.wait_ge(attn_out, n - 1)
                for b, v in enumerate(u["v"]):
                    mm = product(bank(6 + n % 2, DH), probT[:, (n % 2) * 768 + b * P:][:, 0:P], v,
                                 b == 0, b == len(u["v"]) - 1)
                mm.then_inc(pv, 1)

            end = n0 + len(units)
            logits(n0)
            logits(n0 + 1)
            warm(5)
            for n in range(n0, end):
                turn(n)
                if n + 2 < end:
                    logits(n + 2)
                if n > n0:
                    values(n - 1)
            values(end - 1)

        pe.wait_ge(qk_out, 8)
        pe.wait_ge(drained_a, drain_base["v"] + 4)
        pe.wait_ge(hid_ready, NF + 4)
        attention(group1, 0)
        pe.wait_ge(attn_out, len(group1))
        for k in range(4):
            for q in range(ST):
                mm = nc.tensor.transpose(bank(k, P, q * P), attn1[:, q * ATT + k * P:][:, 0:P], ident)
            mm.then_inc(at_T, 1)
        pe.wait_ge(hid_ready, NF + KT)
        feature_tiles("out1", hidH, hidL, (hid_ready, NF))

        up_down("f2", NF + KT, norm_hook(2))

        def before_proj0():
            pe.wait_ge(act_ready, 4 * KT)
            pe.wait_ge(stat_out, 3)

        token_tiles("proj0", 512, 4, before_proj0)
        token_tiles("proj1", 512, 0, lambda: pe.wait_ge(drained_v, drain_base["proj0"]))
        token_tiles("proj2", 512, 4, lambda: pe.wait_ge(drained_v, drain_base["proj1"]))
        pe.wait_ge(drained_v, drain_base["proj2"])
        feature_tiles("gates", actH, actL, (act_ready, 3 * KT), drained=drained_a)

        pe.wait_ge(drained_v, drain_base["merge"])
        pe.wait_ge(q2_rot, 1)
        for n in range(2 * ST):
            if n == ST:
                pe.wait_ge(drained_a, drain_base["gates"] + 16)
            a = (n % ST) * 1536 + (n // ST) * 768
            for pair in range(4):
                mm = nc.tensor.transpose(bank((4 + n) % 8, P, pair * P), nat[:, a + pair * P:][:, 0:P], ident)
            mm.then_inc(q2_T, 1)
        for n in range(2):
            pe.wait_ge(q2_out, n + 1)
            for q in range(ST):
                mm = nc.tensor.transpose(bank(4 + n, P, q * P), nat[:, q * 1536 + n * 768 + 512:][:, 0:P], ident)
            mm.then_inc(q2_T, 1)
        pe.wait_ge(q2_out, 8)
        pe.wait_ge(k2_out, 8)
        attention(group2, len(group1))
        pe.wait_ge(attn_out, len(group1) + len(group2))
        for k in range(KT):
            src = attnA if k < 4 else attnB
            for q in range(ST):
                mm = nc.tensor.transpose(bank(k, P, q * P), src[:, q * ATT + (k % 4) * P:][:, 0:P], ident)
            mm.then_inc(at_T, 1)

        def merge(i):
            for j in range(SLOTS):
                pe.wait_ge(lo_ready, i * 4 + (stage_of["merge"]["base"] + j + 1))
                pe.wait_ge(drained_v, i * 4 + (drain_base["merge"] + j - 3))
                for k in range(KT):
                    if j == 0:
                        pe.wait_ge(act_ready, 4 * KT + KT)
                    a = j * SLAB + k * P
                    mm = split_product(bank(j + 4 * (k // 4)), wH[:, a:a + P], wL[:, a:a + P],
                                       actH[:, k * S:(k + 1) * S], actL[:, k * S:(k + 1) * S], k % 4 == 0, k % 4 == 3)
                mm.then_inc(slab_done, 1)
        loop(pe, 0, 2, merge)
        feature_tiles("out2", hidH, hidL, (hid_ready, 2 * (NF + KT) - KT))

        def layer_norm(n, m):
            pe.wait_ge(acc_done, ACC_TOTAL[n] - KT)
            product(bank(4), ones[:], acc[:], True, True).then_inc(mean_sum, 1)
            row_sums(n)
            spread_rows(n)

        pe.wait_ge(drained_v, drain_base["f3_up0"])
        layer_norm(3, 0)
        up_down("f3", 2 * (NF + KT), None)
        layer_norm(4, 1)

        for k in range(KT):
            pe.wait_ge(fin_ready, k + 1)
            for q in range(ST):
                mm = nc.tensor.transpose(bank(2 * q + k // 4, P, (k % 4) * P), x[:, k * S + q * P:][:, 0:P], ident)
            mm.then_inc(fin_T, 1)

    @block.scalar
    def _(act):
        chain = Chain(act, a_step)
        link = chain.link
        act.dma_start(const[:], t["const"]).then_inc(const_in, 16)
        act.wait_ge(cleared, 1)
        for name, src in vec_sources:
            g, first, n = VEC[name]
            act.dma_start(vec_rows[first:first + n, g * P:(g + 1) * P],
                          src.rearrange("(r c) -> r c", c=P)).then_inc(vec_in, 16)

        def load_mod(chunk, first=False):
            for half in range(2):
                if not first:
                    act.wait_ge(mod_half, chunk * 2 + (half - 1))
                act.dma_start(mod_raw[:, half * 2048:(half + 1) * 2048].rearrange("p (k n) -> p k n", k=4),
                              kview(t["w_mod_2"][0])[:, 4 * half:4 * half + 4, bass.ds(chunk * 512, 512)]
                              ).then_inc(mod_in[half], 16)

        load_mod(0, first=True)
        for dst, src in ((gain1[:, 0:DH], t["q_norm"]), (gain1[:, DH:], t["k_norm"]),
                         (gain2[:, 0:DH], t["q_norm_g_2"]), (gain2[:, DH:], t["k_norm_g_2"]),
                         (sink[:, 0:NH], t["attn_sink_2"]),
                         (biasx[:, 0:256], t["b_in_2"][:, 512:768]), (biasx[:, 256:512], t["b_in_2"][:, 1280:1536])):
            act.dma_start(dst, src.broadcast_to([P, src.shape[1]])).then_inc(misc_in, 16)
        act.dma_start(ctx_nat[:].rearrange("p (q d) -> p q d", q=CT),
                      t["ctx_2"][0].rearrange("(q p) d -> p q d", p=P)).then_inc(ctx_in, 16)

        def split(st, i, j):
            if st is None:
                return
            a, w = j * SLAB, st["width"]
            act.wait_ge(raw_in[j], i * (16 * st["dmas"]) + 16 * (st["raw"] + st["dmas"]))
            if st["name"] != "f1_up0" or not isinstance(i, int):
                act.wait_ge(slab_done, i * 4 + (st["base"] + j - 3))
            nc.scalar.activation(wH[:, a:a + w], raw[:, a:a + w], ACT.Copy).then_inc(hi_ready, 1)

        def slabs(name, per, drain, finish=None):
            st = stage_of[name]

            def body(i, then, k):
                for j in range(SLOTS):
                    drain(i, j)
                    split(then, k, j)
                if finish:
                    finish(i)
            chain.loop(0, st["its"] - 1, per, lambda i: body(i, st, i + 1))
            links = chain.links
            body(st["its"] - 1, nxt.get(name), 0)
            assert chain.links - links == per

        act.wait_ge(cols_ready, 1)
        for k in range(KT):
            act.wait_ge(drained_v, k + 1)
            nc.scalar.activation(tile(actH, k), tile(x, k), ACT.Copy, scale=col("ffn1_norm", k)).then_inc(act_hi, 1)
            if k:
                act.wait_ge(acc_done, k)
            nc.scalar.activation(sq[:], tile(x, k), ACT.Square).then_inc(sq_ready, 1)
            if k % 2:
                split(stage_of["f1_up0"], 0, k // 2)
        for n, name in enumerate(("c", "c_ctx")):
            nc.scalar.activation(silu_c[:, 8 * n:8 * n + 8], cols[:, VEC[name][0] * P + VEC[name][1]:][:, 0:8],
                                 ACT.Silu).then_inc(silu_c_ready, 1)

        def nothing(i, j):
            pass

        def silu(name):
            def drain(i, j):
                if j % 2 == 0:
                    act.wait_ge(drained_v, i * 4 + (drain_base[name] + j + 1))
                    nc.scalar.activation(sg[:], g1[:], ACT.Silu).then_inc(silu_ready, 1)
            return drain

        def normed(name, gain, acc0):
            def drain(i, j):
                m = i * 4 + j
                act.wait_ge(drained_v, i * 4 + (drain_base[name] + j + 1))
                nc.scalar.activation(tile(actH, m), tile(x, m), ACT.Copy, scale=col(gain, m)).then_inc(act_hi, 1)
                act.wait_ge(acc_done, i * 4 + (acc0 + j))
                nc.scalar.activation(sq[:], tile(x, m), ACT.Square).then_inc(sq_ready, 1)
            return drain

        for n in range(len(PARTS)):
            slabs(f"f1_up{n}", 0, silu(f"f1_up{n}"), lambda i, n=n: load_mod(i + (4 * n + 1)))
            slabs(f"f1_down{n}", 0, nothing if n < 2 else normed("f1_down2", "mix_norm", ACC_TOTAL[0]))
        slabs("ctxkv", 0, nothing)

        def token_stage(name, bank0, into, width, wait=None):
            st = stage_of[name]
            for j in range(SLOTS - 1):
                split(nxt[name], 0, j)
            act.wait_ge(slab_done, st["base"] + SLOTS)
            act.wait_ge(rn_ready, 2)
            if wait:
                act.wait_ge(*wait)
            for q in range(ST):
                nc.scalar.activation(into[:, q * width:(q + 1) * width], bank(bank0 + q, width), ACT.Copy,
                                     scale=rn[:, q:q + 1]).then_inc(drained_a, 1)
            split(nxt[name], 0, SLOTS - 1)

        def head_squares(src, n):
            act.wait_ge(drained_a, drain_base[("q", "k")[n]] + 4)
            for q in range(ST):
                for head in range(NH):
                    a = head * DH
                    ins = nc.scalar.activation(rel[:, (q % 2) * S + a:][:, 0:DH], src[:, q * ATT + a:][:, 0:DH],
                                               ACT.Square, accum_out=ssq[:, n * 32 + q * NH + head:][:, 0:1])
                    if head < NH - 1:
                        continue
                    if q < ST - 1:
                        link(ins)
                    else:
                        ins.then_inc(qk_sq, 1)
                        act.wait_ge(qk_sq, n + 1)

        token_stage("idx", 4, pi, IDX_COLS)

        for j in range(SLOTS):
            act.wait_ge(slab_done, stage_of["pool"]["base"] + j + 1)
            nc.scalar.activation(tile(u_pool, j), bank(j), ACT.Copy).then_inc(drained_a, 1)
            split(stage_of["q"], 0, j)
        for n in range((ST - 1) * IDX_HEADS):
            w = P * (n // IDX_HEADS + 2)
            act.wait_ge(idx_qk, n + 1)
            if n >= 2:
                act.wait_ge(idx_rel_used, n - 1)
            nc.scalar.activation(rel[:, (n % 2) * S:][:, 0:w], bank(4 + n % 4, w), ACT.Relu).then_inc(idx_rel, 1)
        token_stage("q", 4, q1, ATT)
        act.wait_ge(idx_rel_used, 12)
        head_squares(q1, 0)
        token_stage("k", 0, k1, ATT)
        head_squares(k1, 1)
        token_stage("v", 4, v1, ATT)

        for g in range(4):
            act.wait_ge(pool_mm, g + 1)
            nc.scalar.activation(tile(hidH, 4 + g), bank(4 + g), ACT.Copy, scale=col("pool_scale", g)).then_inc(pool_hi, 1)
        for n in range(2 * ST):
            into, q = (qT1, kT1)[n // ST], n % ST
            act.wait_ge(qk_T, n + 1)
            nc.scalar.activation(into[:].rearrange("p (a s) -> p a s", a=4)[:, :, q * P:(q + 1) * P],
                                 bank(n % 4).rearrange("p (a s) -> p a s", a=4), ACT.Copy).then_inc(qk_out, 1)

        def attention(units, n0):
            def exps(n):
                u = units[n - n0]
                act.wait_ge(logit, n + 1)
                c = n % 32
                if u["sink"] is not None:
                    link(nc.scalar.activation(stat[:, 64 + c:65 + c], stat[:, c:c + 1], ACT.Exp,
                                              bias=sink[:, u["sink"]:u["sink"] + 1]))
                p = prob[:, (n % 3) * 768:][:, 0:u["W"]]
                nc.scalar.activation(p, p, ACT.Exp, scale=-1.0, bias=stat[:, c:c + 1],
                                     accum_out=stat[:, 32 + c:33 + c]).then_inc(probs, 1)

            def copy(n):
                u = units[n - n0]
                w = min(512, u["W"])
                act.wait_ge(prob_T, n + 1)
                if n >= 2:
                    act.wait_ge(pv, n - 1)
                nc.scalar.activation(probT[:, (n % 2) * 768:][:, 0:w], bank(4, w), ACT.Copy).then_inc(probT_a, 1)

            end = n0 + len(units)
            exps(n0)
            for n in range(n0, end):
                copy(n)
                if n + 1 < end:
                    exps(n + 1)

        attention(group1, 0)
        for k in range(4):
            act.wait_ge(at_T, k + 1)
            nc.scalar.activation(tile(hidH, k), bank(k), ACT.Copy).then_inc(at_hi, 1)

        slabs("out1", 0, normed("out1", "ffn2_norm", ACC_TOTAL[1]))

        def modulated(i, j):
            m = i * 4 + j
            act.wait_ge(drained_v, i * 4 + (drain_base["f2_down2"] + j + 1))
            nc.scalar.activation(tile(actH, m), tile(x, m), ACT.Identity, scale=modc[:, bass.ds(m + 8, 1)],
                                 bias=modc[:, bass.ds(m, 1)]).then_inc(act_hi, 1)

        for n in range(len(PARTS)):
            slabs(f"f2_up{n}", 0, silu(f"f2_up{n}"))
            slabs(f"f2_down{n}", 0, nothing if n < 2 else modulated)
        for g in range(3):
            slabs(f"proj{g}", 0, nothing)

        def gate(i, j):
            act.wait_ge(slab_done, i * 4 + (stage_of["gates"]["base"] + j + 1))
            nc.scalar.activation(tile(gates, i * 4 + j), bank(j), ACT.Sigmoid,
                                 bias=col("b_gate", i * 4 + j)).then_inc(drained_a, 1)

        slabs("gates", 0, gate)
        for n in range(2 * ST):
            into, q = (qTA, qTB)[n // ST], n % ST
            act.wait_ge(q2_T, n + 1)
            nc.scalar.activation(into[:].rearrange("p (a s) -> p a s", a=4)[:, :, q * P:(q + 1) * P],
                                 bank((4 + n) % 8).rearrange("p (a s) -> p a s", a=4), ACT.Copy).then_inc(q2_out, 1)
        attention(group2, len(group1))
        for k in range(KT):
            act.wait_ge(at_T, 4 + k + 1)
            nc.scalar.activation(tile(actH, k), bank(k), ACT.Copy).then_inc(at_hi, 1)
        slabs("merge", 0, nothing)
        slabs("out2", 0, nothing)

        def centred_squares(n):
            for k in range(KT):
                act.wait_ge(centred, n * KT + k + 1)
                if k >= 2:
                    act.wait_ge(acc_done, ACC_TOTAL[3 + n] - KT + k - 1)
                nc.scalar.activation(tile(sq2, k % 2), tile(x, k), ACT.Square).then_inc(sq_ready, 1)

        centred_squares(0)
        for k in range(KT):
            act.wait_ge(scaled, k + 1)
            nc.scalar.activation(tile(actH, k), tile(x, k), ACT.Identity, scale=ln_col[:, k:k + 1],
                                 bias=ln_col[:, KT + k:KT + k + 1]).then_inc(act_hi, 1)

        def conv(name, n0):
            def drain(i, j):
                chan = i * 2 + (PARTS[n0][0] + j // 2 + (NF if j % 2 else 0))
                buf = (cg, cu)[j % 2][:, (j // 2) * S:(j // 2 + 1) * S]
                act.wait_ge(slab_done, i * 4 + (stage_of[name]["base"] + j + 1))
                act.wait_ge(hid_ready, i * 2 + (2 * (NF + KT) + PARTS[n0][0] + j // 2 - 1))
                nc.scalar.activation(buf, bank(j), ACT.Identity, scale=col("conv_w1", chan),
                                     bias=col("conv_b", chan)).then_inc(conv_c, 1)
                if j % 2:
                    gbuf = cg[:, (j // 2) * S:(j // 2 + 1) * S]
                    act.wait_ge(drained_v, i * 4 + (drain_base[name] + j))
                    nc.scalar.activation(gbuf, gbuf, ACT.Silu).then_inc(silu_ready, 1)
            return drain

        for n in range(len(PARTS)):
            slabs(f"f3_up{n}", 0, conv(f"f3_up{n}", n))
            slabs(f"f3_down{n}", 0, nothing)
        centred_squares(1)
        for n in range(6):
            half, q = n // ST, n % ST
            act.wait_ge(fin_T, 4 * (half + 1))
            nc.scalar.activation(out_nat[:, q * D + half * 512:][:, 0:512], bank(2 * q + half), ACT.Copy).then_inc(fin_out, 1)

    @block.vector
    def _(dve):
        chain = Chain(dve, v_step)
        link = chain.link
        V = nc.vector

        def rsqrt(out, v, w, last=None):
            a = small[:, 64:64 + w]
            link(V.tensor_scalar(out.bitcast(I32), v.bitcast(I32), 1, None, ALU.logical_shift_right))
            link(V.tensor_scalar(out.bitcast(I32), out.bitcast(I32), -1.0, RSQRT_MAGIC, ALU.mult, ALU.add))
            for step in range(3):
                link(V.tensor_tensor(a, out, out, ALU.mult))
                link(V.scalar_tensor_tensor(a, a, -0.5, v, ALU.mult, ALU.mult))
                ins = V.scalar_tensor_tensor(out, a, 1.5, out, ALU.add, ALU.mult)
                if step == 2 and last is not None:
                    ins.then_inc(last[0], 1)
                    dve.wait_ge(*last)
                else:
                    link(ins)

        def row_scale(n, eps):
            dve.wait_ge(row_sum, n + 1)
            link(V.tensor_scalar(small[:, 0:ST], bank(4, ST), eps, None, ALU.add))
            rsqrt(rn[:], small[:, 0:ST], ST, last=(rn_ready, n + 1))
            dve.wait_ge(row_bcast, n + 1)
            V.tensor_copy(rB[:], bank(5)).then_inc(stat_out, 1)
            dve.wait_ge(stat_out, n + 1)

        def add_term(term, count):
            V.tensor_tensor(acc[:], acc[:], term, ALU.add).then_inc(acc_done, 1)
            dve.wait_ge(acc_done, count)

        dve.wait_ge(vec_T, 1)
        V.tensor_copy(cols[:], bank(7)).then_inc(cols_ready, 1)
        dve.wait_ge(cols_ready, 1)
        link(V.memset(acc[:], 0.0))
        for k in range(KT):
            dve.wait_ge(xT, k + 1)
            V.tensor_copy(tile(x, k), bank(k % 4)).then_inc(drained_v, 1)
            dve.wait_ge(drained_v, k + 1)
            dve.wait_ge(act_hi, k + 1)
            V.scalar_tensor_tensor(tile(actL, k), tile(x, k), col("ffn1_norm", k), tile(actH, k).bitcast(F32),
                                   ALU.mult, ALU.subtract).then_inc(act_ready, 1)
            dve.wait_ge(sq_ready, k + 1)
            add_term(sq[:], k + 1)
        dve.wait_ge(silu_c_ready, 2)
        row_scale(0, RMS_EPS)

        def mod_products(chunk, half, ctx_too):
            dve.wait_ge(mod_in[half], chunk * 16 + 16)
            n = 2 if ctx_too else 1
            for kk in range(4):
                w = mod_raw[:, (half * 4 + kk) * 512:][:, 0:512]
                for m in range(n):
                    k = half * 4 + kk
                    o, s = mod_acc[:, m * 512:(m + 1) * 512], silu_c[:, m * 8 + k:m * 8 + k + 1]
                    if k == 0:
                        ins = V.tensor_scalar(o, w, s, None, ALU.mult)
                    else:
                        ins = V.scalar_tensor_tensor(o, w, s, o, ALU.mult, ALU.add)
                    if kk < 3 or m < n - 1:
                        link(ins)
            ins.then_inc(mod_half, 1)
            dve.wait_ge(mod_half, chunk * 2 + (half + 1))

        def mod_columns(chunk, ctx_too):
            dve.wait_ge(mod_sum, chunk + 1)
            b = cols[:, bass.ds(chunk * 4 + VEC["b_mod"][1], 4)]
            if ctx_too:
                link(V.tensor_tensor(modx[:, bass.ds(chunk * 4, 4)], bank(6, 4, 4), b, ALU.add))
            V.tensor_tensor(modc[:, bass.ds(chunk * 4, 4)], bank(6, 4), b, ALU.add).then_inc(mod_cols, 1)
            dve.wait_ge(mod_cols, chunk + 1)

        def hidden(name, i, q, hid0):
            st, d0 = stage_of[name], drain_base[name]
            f = i * 2 + q
            dve.wait_ge(slab_done, i * 4 + (st["base"] + 2 * q + 1))
            V.tensor_tensor(g1[:], bank(2 * q), rB[:], ALU.mult).then_inc(drained_v, 1)
            dve.wait_ge(slab_done, i * 4 + (st["base"] + 2 * q + 2))
            V.tensor_tensor(ur[:], bank(2 * q + 1), rB[:], ALU.mult).then_inc(drained_v, 1)
            dve.wait_ge(drained_v, i * 4 + (d0 + 2 * q + 2))
            dve.wait_ge(silu_ready, f + (SILU_BEFORE[name] + 1))
            link(V.tensor_tensor(h[:], sg[:], ur[:], ALU.mult))
            link(V.tensor_scalar(tile(hidH, f), h[:], 1.0, None, ALU.mult))
            V.tensor_tensor(tile(hidL, f), h[:], tile(hidH, f).bitcast(F32), ALU.subtract).then_inc(hid_ready, 1)
            dve.wait_ge(hid_ready, f + (hid0 + 1))

        def add_down(name):
            st, d0 = stage_of[name], drain_base[name]

            def body(i):
                for j in range(SLOTS):
                    m = i * 4 + j
                    dve.wait_ge(slab_done, i * 4 + (st["base"] + j + 1))
                    V.scalar_tensor_tensor(tile(x, m), bank(j), 0.5, tile(x, m), ALU.mult, ALU.add).then_inc(drained_v, 1)
            chain.loop(0, 2, 0, body)
            dve.wait_ge(drained_v, d0 + KT)

        def last_down(name, scale, gain, act0, hi0, sq0, acc0):
            st, d0 = stage_of[name], drain_base[name]
            link(V.memset(acc[:], 0.0))

            def body(i):
                for j in range(SLOTS):
                    m = i * 4 + j
                    dve.wait_ge(slab_done, i * 4 + (st["base"] + j + 1))
                    V.scalar_tensor_tensor(tile(x, m), bank(j), scale, tile(x, m), ALU.mult, ALU.add).then_inc(drained_v, 1)
                    dve.wait_ge(drained_v, i * 4 + (d0 + j + 1))
                    dve.wait_ge(act_hi, i * 4 + (hi0 + j + 1))
                    V.scalar_tensor_tensor(tile(actL, m), tile(x, m), col(gain, m), tile(actH, m).bitcast(F32),
                                           ALU.mult, ALU.subtract).then_inc(act_ready, 1)
                    dve.wait_ge(sq_ready, i * 4 + (sq0 + j + 1))
                    add_term(sq[:], i * 4 + (acc0 + j + 1))
            chain.loop(0, 2, 0, body)
            dve.wait_ge(act_ready, act0 + KT)

        for n, (f0, nf) in enumerate(PARTS):
            def body(i, n=n, f0=f0):
                chunk = i + 4 * n
                for q in range(2):
                    mod_products(chunk, q, n == 0)
                    hidden(f"f1_up{n}", i, q, f0)
                mod_columns(chunk, n == 0)
            chain.loop(0, nf // 2, 2 * ((7 if n == 0 else 3) + 2) + (1 if n == 0 else 0), body)
            if n == 2:
                mod_products(11, 0, False)
                mod_products(11, 1, False)
                link(V.tensor_scalar(modx[:, 8:16], modx[:, 8:16], 1.0, None, ALU.add))
                for k in range(KT):
                    dve.wait_ge(ctx_T, k + 1)
                    V.tensor_scalar(h[:, 0:CTX], bank(4 + k % 4, CTX), modx[:, 8 + k:9 + k], modx[:, k:k + 1],
                                    ALU.mult, ALU.add).then_inc(ctx_drained, 1)
                    dve.wait_ge(ctx_drained, k + 1)
                    link(V.tensor_copy(tile(hcH, k, CTX), h[:, 0:CTX]))
                    V.tensor_tensor(tile(hcL, k, CTX), h[:, 0:CTX], tile(hcH, k, CTX).bitcast(F32),
                                    ALU.subtract).then_inc(hc_ready, 1)
                    dve.wait_ge(hc_ready, k + 1)
            if n < 2:
                add_down(f"f1_down{n}")
            else:
                last_down("f1_down2", 0.5, "mix_norm", KT, KT, KT, ACC_TOTAL[0])

        mod_columns(11, False)
        link(V.tensor_scalar(modc[:, 8:16], modc[:, 8:16], 1.0, None, ALU.add))
        link(V.tensor_scalar(modc[:, 32:40], modc[:, 32:40], 1.0, None, ALU.add))
        row_scale(1, RMS_EPS)

        dve.wait_ge(misc_in, MISC_DMAS * 16)
        kc = kctx[:].rearrange("p (n d) -> p n d", n=4)
        for g, v in ((0, vA), (1, vB)):
            dve.wait_ge(slab_done, stage_of["ctxkv"]["base"] + 2 * g + 2)
            for q in range(CT):
                b = 2 * g + q
                link(V.tensor_tensor(kc[:, b, :], bank(b, P), biasx[:, g * 256:g * 256 + P], ALU.add))
                V.tensor_tensor(v[:, q * P:(q + 1) * P], bank(b, P, P), biasx[:, g * 256 + P:g * 256 + 256],
                                ALU.add).then_inc(drained_v, 1)
        dve.wait_ge(drained_v, drain_base["ctxkv"] + 4)
        kb = kctx[:, 2 * P:4 * P].rearrange("p (n d) -> p n d", d=DH)
        tk = tA[:, 0:2 * P].rearrange("p (n d) -> p n d", d=DH)
        link(V.tensor_tensor(tk, kb, kb, ALU.mult))
        link(V.tensor_reduce(small[:, 0:4], tk, AX_X, ALU.add))
        link(V.tensor_scalar(small[:, 0:4], small[:, 0:4], 1.0 / DH, QK_EPS, ALU.mult, ALU.add))
        rsqrt(small[:, 128:132], small[:, 0:4], 4)
        link(V.tensor_tensor(kb, kb, small[:, 128:132].unsqueeze(2).broadcast_to([P, 4, DH]), ALU.mult))
        V.tensor_tensor(kb, kb, gain2[:, DH:].unsqueeze(1).broadcast_to([P, 4, DH]), ALU.mult).then_inc(kctx_ready, 2)
        dve.wait_ge(kctx_ready, 2)
        link(V.tensor_scalar(sink[:, NH:], sink[:, 0:NH], -1.0, None, ALU.mult))

        def gained_tables(cos, sin, gain, groups, half):
            for n in range(2):
                g = gain[:, n * DH:(n + 1) * DH]
                c = ropeT[:, 2 * n * ST * DH:][:, 0:ST * DH].rearrange("p (q d) -> p q d", q=ST)
                s = ropeT[:, (2 * n + 1) * ST * DH:][:, 0:ST * DH].rearrange("p (q d) -> p q d", q=ST)
                link(V.tensor_tensor(c, cos.rearrange("p (q d) -> p q d", q=ST),
                                     g.unsqueeze(1).broadcast_to([P, ST, DH]), ALU.mult))
                for r in range(groups):
                    for to, frm in ((0, half), (half, 0)):
                        a = 2 * r * half
                        link(V.tensor_tensor(s[:, :, a + to:a + to + half],
                                             sin.rearrange("p (q d) -> p q d", q=ST)[:, :, a + to:a + to + half],
                                             g[:, a + frm:a + frm + half].unsqueeze(1).broadcast_to([P, ST, half]),
                                             ALU.mult))

        gained_tables(cv("cos1"), cv("sin1"), gain1, 1, DH // 2)

        for q in range(ST):
            dve.wait_ge(drained_a, drain_base["idx"] + q + 1)
            v = pi[:, q * IDX_COLS:][:, 0:(IDX_HEADS + 1) * IDX_DIM].rearrange("p (h d) -> p h d", d=IDX_DIM)[:, :, 0:IDX_ROT]
            tmp = tA[:, 0:(IDX_HEADS + 1) * IDX_ROT].rearrange("p (h d) -> p h d", d=IDX_ROT)
            rotate(V, link, v, tmp, IDX_HEADS + 1, 1, IDX_ROT // 2, cv("cosi")[:, q * IDX_ROT:(q + 1) * IDX_ROT],
                 cv("sini")[:, q * IDX_ROT:(q + 1) * IDX_ROT], last=idx_rot)
            dve.wait_ge(idx_rot, q + 1)
        wi = pi[:].rearrange("p (q c) -> p q c", q=ST)[:, :, IDX_COLS - IDX_HEADS:]
        link(V.tensor_scalar(wi, wi, IDX_SCALE, None, ALU.mult))
        dve.wait_ge(idx_T, 1)
        for dst, src in ((qiT[:, 0:S], bank(4)), (qiT[:, S:], bank(5)), (kiT[0:DH, :], ps[0:DH, 6, :]),
                         (kiT[DH:P, :], ps[0:DH, 6, :])):
            V.tensor_copy(dst, src).then_inc(idx_cols, 1)

        def mask_of(q):
            return work[:, P * (q * (q + 1) // 2 - 1):][:, 0:P * (q + 1)]

        for n in range((ST - 1) * IDX_HEADS):
            q, head = n // IDX_HEADS + 1, n % IDX_HEADS
            w, m = P * (q + 1), mask_of(q)
            r, c = rel[:, (n % 2) * S:][:, 0:w], pi[:, q * IDX_COLS + IDX_COLS - IDX_HEADS + head:][:, 0:1]
            dve.wait_ge(idx_rel, n + 1)
            if head == 0:
                V.tensor_scalar(m, r, c, None, ALU.mult).then_inc(idx_rel_used, 1)
            else:
                V.scalar_tensor_tensor(m, r, c, m, ALU.mult, ALU.add).then_inc(idx_rel_used, 1)
            dve.wait_ge(idx_rel_used, n + 1)
            if head == IDX_HEADS - 1:
                link(V.tensor_tensor(m[:, q * P:], m[:, q * P:], cv("causal"), ALU.add))

        def pick(q, first=0, end=TOPK // 8):
            m, top = mask_of(q), small[:, 0:8]
            for _ in range(first, end):
                link(V.max(top, m))
                link(V.match_replace(m, top, m, TAKEN))
            if end == TOPK // 8:
                link(V.tensor_scalar(m, m, TAKEN / 1.5, NEG, ALU.is_gt, ALU.mult))

        pick(1)

        pick(2)

        def head_scales(n, out, last=None):
            dve.wait_ge(qk_sq, n + 1)
            link(V.tensor_scalar(small[:, 0:32], ssq[:, n * 32:n * 32 + 32], 1.0 / DH, RMS_EPS, ALU.mult, ALU.add))
            rsqrt(out, small[:, 0:32], 32, last=last)

        def spread_keys(kT, src, a, w, done):
            for kv in range(NKV):
                for half in range(2):
                    c = kv * (CTX + S) + a
                    V.tensor_copy(kT[half * DH:(half + 1) * DH, c:c + w],
                                  src[kv * DH:(kv + 1) * DH, :]).then_inc(done, 1)

        head_scales(0, small[:, 128:160])
        heads_rotated(V, chain, q1, 0, tA, small[:, 128:160], qk_rot)
        head_scales(1, k_scale[:], last=(k_scaled, 1))
        pick(3, 0, 5)
        dve.wait_ge(kctx_T, 1)
        spread_keys(kTA, ps[:, 0, 0:CTX], 0, CTX, kctx_out)
        spread_keys(kTB, ps[:, 0, CTX:2 * CTX], 0, CTX, kctx_out)
        for g in range(4):
            dve.wait_ge(pool_hi, g + 1)
            V.scalar_tensor_tensor(tile(hidL, 4 + g), bank(4 + g), col("pool_scale", g), tile(hidH, 4 + g).bitcast(F32),
                                   ALU.mult, ALU.subtract).then_inc(hid_ready, 1)

        pick(3, 5)

        def attention(units, n0):
            def logits(n):
                u, c = units[n - n0], n % 32
                dve.wait_ge(att_qk, n + 1)
                if n >= 3:
                    dve.wait_ge(prob_T, n - 2)
                b = 2 * (n % 2)
                src = ps[:, b:b + 2, :].rearrange("p b n -> p (b n)")[:, 0:u["W"]]
                start = 3e38 if u["sink"] is None else sink[:, NH + u["sink"]:][:, 0:1]
                V.tensor_tensor_reduce(out=prob[:, (n % 3) * 768:][:, 0:u["W"]], in0=src, in1=u["mask"],
                                       scale=-(DH ** -0.5), scalar=start, op0=ALU.add, op1=ALU.min,
                                       accum_out=stat[:, c:c + 1]).then_inc(logit, 1)

            def sums(n):
                u, c = units[n - n0], n % 32
                dve.wait_ge(probs, n + 1)
                total = stat[:, 32 + c:33 + c]
                if u["sink"] is not None:
                    link(V.tensor_tensor(total, total, stat[:, 64 + c:65 + c], ALU.add))
                link(V.reciprocal(stat[:, 96 + c:97 + c], total))

            def copy(n):
                u = units[n - n0]
                if u["W"] > 512:
                    dve.wait_ge(prob_T, n + 1)
                    dve.wait_ge(pv, n - 1)
                    V.tensor_copy(probT[:, (n % 2) * 768 + 512:][:, 0:u["W"] - 512],
                                  bank(5, u["W"] - 512)).then_inc(probT_v, 1)

            def out(n):
                u, c = units[n - n0], n % 32
                dve.wait_ge(pv, n + 1)
                V.tensor_scalar(u["out"], bank(6 + n % 2, DH), stat[:, 96 + c:97 + c], None, ALU.mult).then_inc(attn_out, 1)

            end = n0 + len(units)
            logits(n0)
            logits(n0 + 1)
            for n in range(n0, end):
                copy(n)
                if n + 2 < end:
                    logits(n + 2)
                sums(n)
                if n > n0:
                    out(n - 1)
            out(end - 1)

        attention(group1, 0)
        for k in range(4):
            dve.wait_ge(at_hi, k + 1)
            V.tensor_tensor(tile(hidL, k), bank(k), tile(hidH, k).bitcast(F32), ALU.subtract).then_inc(hid_ready, 1)
        last_down("out1", 1.0, "ffn2_norm", 2 * KT, 2 * KT, 2 * KT, ACC_TOTAL[1])
        row_scale(2, RMS_EPS)

        for n, (f0, nf) in enumerate(PARTS):
            chain.loop(0, nf // 2, 4, lambda i, n=n, f0=f0: [hidden(f"f2_up{n}", i, q, NF + KT + f0) for q in range(2)])
            if n < 2:
                add_down(f"f2_down{n}")
        st, d0 = stage_of["f2_down2"], drain_base["f2_down2"]

        def modulated(i):
            for j in range(SLOTS):
                m = i * 4 + j
                dve.wait_ge(slab_done, i * 4 + (st["base"] + j + 1))
                V.scalar_tensor_tensor(tile(x, m), bank(j), 0.5, tile(x, m), ALU.mult, ALU.add).then_inc(drained_v, 1)
                dve.wait_ge(drained_v, i * 4 + (d0 + j + 1))
                link(V.tensor_scalar(h[:], tile(x, m), modc[:, bass.ds(m + 8, 1)], modc[:, bass.ds(m, 1)],
                                     ALU.mult, ALU.add))
                dve.wait_ge(act_hi, i * 4 + (3 * KT + j + 1))
                V.tensor_tensor(tile(actL, m), h[:], tile(actH, m).bitcast(F32), ALU.subtract).then_inc(act_ready, 1)
                dve.wait_ge(act_ready, i * 4 + (3 * KT + j + 1))
        chain.loop(0, 2, 4, modulated)
        gained_tables(cv("cos2"), cv("sin2"), gain2, 2, DH // 4)

        dve.wait_ge(bias_in, 16)
        for g in range(3):
            dve.wait_ge(slab_done, stage_of[f"proj{g}"]["base"] + SLOTS)
            for q in range(ST):
                V.tensor_tensor(nat[:, q * 1536 + g * 512:][:, 0:512], bank((4, 0, 4)[g] + q),
                                bias2[:, g * 512:(g + 1) * 512], ALU.add).then_inc(drained_v, 1)
        dve.wait_ge(drained_v, drain_base["merge"])
        HB = NH + NKV
        for q in range(ST):
            a = q * 1536
            xa = nat[:, a:a + HB * DH].rearrange("p (h d) -> p h d", d=DH)
            tmp = tC[:, 0:HB * DH].rearrange("p (h d) -> p h d", d=DH)
            rotate(V, link, xa, tmp, HB, 2, DH // 4, cv("cos2")[:, q * DH:(q + 1) * DH], cv("sin2")[:, q * DH:(q + 1) * DH])
            xb = nat[:, a + 768:a + 768 + HB * DH].rearrange("p (h d) -> p h d", d=DH)
            link(V.tensor_tensor(tmp, xb, xb, ALU.mult))
            link(V.tensor_reduce(ssq[:, q * HB:(q + 1) * HB], tmp, AX_X, ALU.add))
            link(V.tensor_copy(vA[:, (CT + q) * P:(CT + q + 1) * P], nat[:, a + 640:a + 768]))
            link(V.tensor_copy(vB[:, (CT + q) * P:(CT + q + 1) * P], nat[:, a + 1408:a + 1536]))
        link(V.tensor_scalar(small[:, 0:ST * HB], ssq[:, 0:ST * HB], 1.0 / DH, QK_EPS, ALU.mult, ALU.add))
        rsqrt(small[:, 128:128 + ST * HB], small[:, 0:ST * HB], ST * HB)
        for q in range(ST):
            a = q * 1536 + 768
            xb = nat[:, a:a + HB * DH].rearrange("p (h d) -> p h d", d=DH)
            link(V.tensor_tensor(xb, xb, small[:, 128 + q * HB:][:, 0:HB].unsqueeze(2).broadcast_to([P, HB, DH]),
                                 ALU.mult))
            for n, first, heads in ((0, 0, NH), (1, NH, NKV)):
                last = q2_rot if q == ST - 1 and n == 1 else None
                rotate(V, link, xb[:, first:first + heads, :], tC[:, 0:heads * DH].rearrange("p (h d) -> p h d", d=DH),
                     heads, 2, DH // 4, gained(n, 0, q), gained(n, 1, q), last=last)
        for n, kT in enumerate((kTA, kTB)):
            dve.wait_ge(q2_T, 8 + n + 1)
            spread_keys(kT, bank(4 + n), CTX, S, k2_out)

        attention(group2, len(group1))
        for k in range(KT):
            dve.wait_ge(at_hi, 4 + k + 1)
            V.tensor_tensor(tile(actL, k), bank(k), tile(actH, k).bitcast(F32), ALU.subtract).then_inc(act_ready, 1)

        def merge(i):
            for j in range(SLOTS):
                m = i * 4 + j
                dve.wait_ge(slab_done, i * 4 + (stage_of["merge"]["base"] + j + 1))
                link(V.tensor_tensor(mA[:], bank(j), tile(gates, m), ALU.mult))
                V.tensor_tensor(mB[:], bank(4 + j), tile(gates, m + 8), ALU.mult).then_inc(drained_v, 1)
                dve.wait_ge(drained_v, i * 4 + (drain_base["merge"] + j + 1))
                link(V.tensor_tensor(mA[:], mA[:], mB[:], ALU.add))
                link(V.tensor_scalar(tile(hidH, m), mA[:], 1.0, None, ALU.mult))
                V.tensor_tensor(tile(hidL, m), mA[:], tile(hidH, m).bitcast(F32), ALU.subtract).then_inc(hid_ready, 1)
                dve.wait_ge(hid_ready, i * 4 + (2 * NF + KT + j + 1))
        chain.loop(0, 2, 12, merge)

        def residual(name, gate0, buf, scale, acc0):
            s, d = stage_of[name], drain_base[name]
            if acc0 is not None:
                link(V.memset(acc[:], 0.0))

            def body(i):
                for j in range(SLOTS):
                    m = i * 4 + j
                    dve.wait_ge(slab_done, i * 4 + (s["base"] + j + 1))
                    V.tensor_scalar(buf[:], bank(j), modc[:, bass.ds(m + gate0, 1)], None, ALU.mult).then_inc(drained_v, 1)
                    dve.wait_ge(drained_v, i * 4 + (d + j + 1))
                    link(V.scalar_tensor_tensor(tile(x, m), tile(x, m), scale, buf[:], ALU.mult, ALU.add))
                    if acc0 is not None:
                        add_term(tile(x, m), i * 4 + (acc0 + j + 1))
            chain.loop(0, 2, 4, body)

        def layer_norm(n):
            total = ACC_TOTAL[3 + n] - KT
            dve.wait_ge(mean_sum, n + 1)
            link(V.memset(acc[:], 0.0))
            for k in range(KT + 1):
                if k < KT:
                    V.tensor_tensor(tile(x, k), tile(x, k), bank(4), ALU.subtract).then_inc(centred, 1)
                if k:
                    dve.wait_ge(sq_ready, 3 * KT + n * KT + k)
                    add_term(tile(sq2, (k - 1) % 2), total + k)
            dve.wait_ge(centred, (n + 1) * KT)
            row_scale(3 + n, LN_EPS)

        residual("out2", 16, mA, ALPHA, ACC_TOTAL[2])
        s2 = modc[:, 32:40]
        g0, b0 = (cols[:, VEC[n][1]:VEC[n][1] + KT] for n in ("ln1_g", "ln1_b"))
        link(V.tensor_tensor(ln_col[:, 0:KT], g0, s2, ALU.mult))
        link(V.tensor_tensor(ln_col[:, KT:], b0, s2, ALU.mult))
        link(V.tensor_tensor(ln_col[:, KT:], ln_col[:, KT:], modc[:, 24:32], ALU.add))
        layer_norm(0)
        for k in range(KT):
            V.tensor_tensor(tile(x, k), tile(x, k), rB[:], ALU.mult).then_inc(scaled, 1)
            dve.wait_ge(scaled, k + 1)
            link(V.tensor_scalar(mA[:], tile(x, k), ln_col[:, k:k + 1], ln_col[:, KT + k:KT + k + 1], ALU.mult, ALU.add))
            dve.wait_ge(act_hi, 4 * KT + k + 1)
            V.tensor_tensor(tile(actL, k), mA[:], tile(actH, k).bitcast(F32), ALU.subtract).then_inc(act_ready, 1)
            dve.wait_ge(act_ready, 5 * KT + k + 1)
            link(V.tensor_scalar(tile(x, k), tile(x, k), col("ln1_g", k), col("ln1_b", k), ALU.mult, ALU.add))

        def conv(i, n):
            name, (f0, nf) = f"f3_up{n}", PARTS[n]
            s, d = stage_of[name], drain_base[name]
            before = 2 * f0
            for j in range(SLOTS):
                chan = i * 2 + (f0 + j // 2 + (NF if j % 2 else 0))
                buf = (cg, cu)[j % 2][:, (j // 2) * S:(j // 2 + 1) * S]
                dve.wait_ge(conv_c, i * 4 + (before + j + 1))
                link(V.scalar_tensor_tensor(buf[:, 1:S], bank(j, S - 1), col("conv_w0", chan), buf[:, 1:S],
                                            ALU.mult, ALU.add))
                V.scalar_tensor_tensor(buf[:, 0:S - 1], bank(j, S - 1, 1), col("conv_w2", chan), buf[:, 0:S - 1],
                                       ALU.mult, ALU.add).then_inc(drained_v, 1)
                if j % 2:
                    q = j // 2
                    dve.wait_ge(drained_v, i * 4 + (d + j + 1))
                    dve.wait_ge(silu_ready, i * 2 + (2 * NF + f0 + q + 1))
                    link(V.tensor_tensor(h3[:], cg[:, q * S:(q + 1) * S], buf, ALU.mult))
                    link(V.tensor_scalar(tile(hidH, i * 2 + q), h3[:], 1.0, None, ALU.mult))
                    V.tensor_tensor(tile(hidL, i * 2 + q), h3[:], tile(hidH, i * 2 + q).bitcast(F32),
                                    ALU.subtract).then_inc(hid_ready, 1)
                    dve.wait_ge(hid_ready, i * 2 + (2 * (NF + KT) + f0 + q + 1))

        for n, (f0, nf) in enumerate(PARTS):
            chain.loop(0, nf // 2, 8, lambda i, n=n: conv(i, n))
            residual(f"f3_down{n}", 40, h3, ALPHA if n == 0 else 1.0, ACC_TOTAL[3] if n == 2 else None)

        layer_norm(1)
        for k in range(KT):
            link(V.tensor_tensor(tile(x, k), tile(x, k), rB[:], ALU.mult))
            V.tensor_scalar(tile(x, k), tile(x, k), col("ln2_g", k), col("ln2_b", k), ALU.mult, ALU.add).then_inc(fin_ready, 1)
        dve.wait_ge(fin_T, 8)
        dve.wait_ge(fin_out, 6)
        for q in (2, 3):
            V.tensor_copy(out_nat[:, q * D + 512:][:, 0:512], bank(2 * q + 1)).then_inc(fin_out, 1)


_NAMES = ["x", "ffn1_norm", "ffn1_w_gate", "ffn1_w_up", "ffn1_w_down", "mix_norm", "w_in", "q_norm", "k_norm",
          "pool_w", "pool_scale", "w_out", "ffn2_norm", "ffn2_w_gate", "ffn2_w_up", "ffn2_w_down", "c_2", "ctx_2",
          "c_ctx_2", "w_mod_2", "b_mod_2", "w_in_2", "b_in_2", "attn_sink_2", "q_norm_g_2", "k_norm_g_2",
          "w_branch_a_2", "w_branch_b_2", "w_out_2", "ln1_g_2", "ln1_b_2", "w_up_2", "conv_w_2", "conv_b_2",
          "w_down_2", "ln2_g_2", "ln2_b_2"]


def kernel(**inputs):
    import concourse.bacc as bacc
    from concourse.bass_utils import run_bass_kernel_spmd

    nc = bacc.Bacc("TRN2", target_bir_lowering=False, num_devices=1)
    arrays, t = {}, {}
    for name in _NAMES:
        a = np.ascontiguousarray(inputs[name])
        arrays[f"in_{name}"] = a
        t[name] = nc.dram_tensor(f"in_{name}", a.shape, mybir.dt.from_np(a.dtype), kind="ExternalInput").ap()
    arrays["in_const"] = constants()
    t["const"] = nc.dram_tensor("in_const", (P, N_CONST), F32, kind="ExternalInput").ap()
    t["out"] = nc.dram_tensor("out_0", (1, S, D), F32, kind="ExternalOutput").ap()
    build(nc, t)
    r = run_bass_kernel_spmd(nc, [arrays], core_ids=[0])
    return r.results[0]["out_0"]
```

```python
from contextlib import ExitStack

import numpy as np
import concourse.bass as bass
from concourse import mybir

F32 = mybir.dt.float32
F32R = mybir.dt.float32r
I32 = mybir.dt.int32
ALU = mybir.AluOpType
ACT = mybir.ActivationFunctionType
AX_X = mybir.AxisListType.X

P = 128
D = 1024
S = 512
KT = D // P
ST = S // P
FF = 2816
NF = FF // P
CTX = 256
CT = CTX // P
DH = 64
NH = 8
ATT = NH * DH
NKV = 2
IDX_HEADS, IDX_DIM, IDX_ROT = 4, 64, 32
IDX_COLS = IDX_HEADS * IDX_DIM + IDX_DIM + IDX_HEADS
TOPK = min(256, S // 4)
POOL_WINDOWS = (2, 4, 8, 16)
GRID_W = 64
THETA = 10000.0
RMS_EPS, QK_EPS, LN_EPS = 1e-6, 1e-6, 1e-5
IDX_SCALE = (IDX_HEADS ** -0.5) * (IDX_DIM ** -0.5)
ALPHA = 2.0 ** 0.25
NEG = -1e30
TAKEN = -3e38
RSQRT_MAGIC = float(0x5F3759DF)

PARTS = ((0, 8), (8, 8), (16, 6))
SLOTS = 4
SLAB = 8 * P

CONST = {}
_at = 0
for _name, _w in (("ident", P), ("causal", P), ("band", 7 * P), ("inv_count", 16),
                  ("cos1", ST * DH), ("sin1", ST * DH), ("cosi", ST * IDX_ROT), ("sini", ST * IDX_ROT),
                  ("cos2", ST * DH), ("sin2", ST * DH)):
    CONST[_name] = (_at, _w)
    _at += _w
N_CONST = _at

VEC = {"ffn1_norm": (0, 0, 8), "mix_norm": (0, 8, 8), "ffn2_norm": (0, 16, 8), "b_mod": (0, 24, 48),
       "b_gate": (0, 72, 16), "ln1_g": (0, 88, 8), "ln1_b": (0, 96, 8), "ln2_g": (0, 104, 8),
       "ln2_b": (0, 112, 8), "c": (0, 120, 8), "c_ctx": (1, 0, 8), "pool_scale": (1, 8, 4),
       "conv_b": (1, 12, 44), "conv_w0": (2, 0, 44), "conv_w1": (2, 44, 44), "conv_w2": (3, 0, 44)}


def constants():
    out = np.zeros((P, N_CONST), np.float32)
    row, col = np.arange(P)[:, None], np.arange(P)[None, :]

    def put(name, value):
        a, w = CONST[name]
        out[:, a:a + w] = value.reshape(P, w)

    neg = np.float32(NEG)
    put("ident", (row == col).astype(np.float32))
    put("causal", np.where(col > row, neg, np.float32(0)))
    before = np.where(col >= row, np.float32(0), neg)
    after = np.where(col <= row, np.float32(0), neg)
    zero = np.zeros((P, P), np.float32)
    put("band", np.concatenate([before, zero, after, zero, zero, before, zero], axis=1))
    put("inv_count", np.broadcast_to(1 / (np.arange(16, dtype=np.float32) + 1), (P, 16)))
    pos = np.arange(S, dtype=np.float32).reshape(ST, P).T

    def table(parts):
        cos, sin = [], []
        for where, half in parts:
            inv = np.float32(THETA) ** (-np.arange(half, dtype=np.float32) / np.float32(half))
            ang = (where[:, :, None] * inv).astype(np.float32)
            cos += [np.cos(ang), np.cos(ang)]
            sin += [-np.sin(ang), np.sin(ang)]
        return np.concatenate(cos, axis=2), np.concatenate(sin, axis=2)

    for name, parts in (("1", [(pos, DH // 2)]), ("i", [(pos, IDX_ROT // 2)]),
                        ("2", [(pos // GRID_W, DH // 4), (pos % GRID_W, DH // 4)])):
        cos, sin = table(parts)
        put("cos" + name, cos)
        put("sin" + name, sin)
    return out


class Chain:

    def __init__(self, engine, sem):
        self.engine, self.sem, self.n, self.links = engine, sem, 0, 0

    def link(self, instruction):
        instruction.then_inc(self.sem, 1)
        self.n, self.links = self.n + 1, self.links + 1
        self.engine.wait_ge(self.sem, self.n)

    def loop(self, first, end, per, body):
        if first >= end:
            return
        start, links = self.n, self.links
        if end - first == 1:
            body(first)
        else:
            with self.engine.Fori(first, end) as i:
                self.n = start + (i - first) * per
                body(i)
        assert self.links - links == per, (self.links - links, per)
        self.n = start + (end - first) * per


def loop(engine, first, end, body):
    if end - first == 1:
        body(first)
    elif end > first:
        with engine.Fori(first, end) as i:
            body(i)


def build(nc, t):
    stack = ExitStack()
    with stack:
        _build(nc, t, stack)


def _build(nc, t, stack):
    stages = []

    def stage(name, slabs, width, sources):
        base = sum(s["slabs"] for s in stages)
        dmas = len(sources(0, 0))
        raw = sum(s["slabs"] // SLOTS * s["dmas"] for s in stages)
        stages.append(dict(name=name, slabs=slabs, width=width, sources=sources, base=base,
                           dmas=dmas, raw=raw, its=slabs // SLOTS))

    def kview(w):
        return w.rearrange("(k p) n -> p k n", p=P)

    def ffn(name, gate, up, up_off, down):
        for n, (f0, nf) in enumerate(PARTS):
            stage(f"{name}_up{n}", 2 * nf, SLAB, lambda i, j, f0=f0: [
                (0, kview(gate if j % 2 == 0 else up)[:, :, bass.ds(
                    (i * 2 + (f0 + j // 2)) * P + (up_off if j % 2 else 0), P)])])
            stage(f"{name}_down{n}", KT, nf * P, lambda i, j, f0=f0, nf=nf: [
                (0, kview(down[f0 * P:(f0 + nf) * P, :])[:, :, bass.ds((i * 4 + j) * P, P)])])

    def columns(name, w, first, n):
        stage(name, n, SLAB, lambda i, j: [(0, kview(w)[:, :, bass.ds((i * 4 + j) * P + first, P)])])

    def rows(name, w, first, width, per):
        stage(name, KT // per, per * width, lambda i, j: [
            (0, kview(w)[:, j * per:(j + 1) * per, first:first + width])])

    w_in, w_in2 = t["w_in"][0], t["w_in_2"][0]
    ffn("f1", t["ffn1_w_gate"][0], t["ffn1_w_up"][0], 0, t["ffn1_w_down"][0])
    stage("ctxkv", 4, SLAB, lambda i, j: [(0, kview(w_in2)[:, 4 * (j % 2):4 * (j % 2) + 4,
                                               (512, 1280)[j // 2]:(512, 1280)[j // 2] + 256])])
    rows("idx", w_in, 3 * ATT, IDX_COLS, 2)
    columns("pool", w_in, 3 * ATT + IDX_COLS, 4)
    rows("q", w_in, 0, ATT, 2)
    rows("k", w_in, ATT, ATT, 2)
    rows("v", w_in, 2 * ATT, ATT, 2)
    columns("out1", t["w_out"][0], 0, KT)
    ffn("f2", t["ffn2_w_gate"][0], t["ffn2_w_up"][0], 0, t["ffn2_w_down"][0])
    for g in range(3):
        rows(f"proj{g}", w_in2, 512 * g, 512, 2)
    columns("gates", w_in2, 1536, 16)
    wa, wb = t["w_branch_a_2"][0], t["w_branch_b_2"][0]
    stage("merge", KT, SLAB, lambda i, j: [(0, kview(wa)[:, :, bass.ds((i * 4 + j) * P, P)]),
                                           (4, kview(wb)[:, :, bass.ds((i * 4 + j) * P, P)])])
    columns("out2", t["w_out_2"][0], 0, KT)
    ffn("f3", t["w_up_2"][0], t["w_up_2"][0], FF, t["w_down_2"][0])
    stage_of = {s["name"]: s for s in stages}
    nxt = {a["name"]: b for a, b in zip(stages, stages[1:])}

    by_act = {"idx", "pool", "q", "k", "v", "gates"}
    drain_base, totals = {}, {"v": KT, "a": 0}
    for s in stages:
        who = "a" if s["name"] in by_act else "v"
        drain_base[s["name"]] = totals[who]
        totals[who] += s["slabs"]

    def sb(name, cols, dt=F32):
        return stack.enter_context(nc.sbuf_tensor(name, [P, cols], dt))

    first_byte = {}

    def region(name, cols):
        first_byte[name] = (nc.sbuf_base, cols * 4)
        return stack.enter_context(nc.sbuf_tensor(name + "_room", [P, cols], F32))

    def at(name, where, cols, dt=F32):
        room, first = where
        base, size = first_byte[room]
        assert (first + cols) * 4 <= size, (name, room)
        return nc.alloc_sbuf_tensor_at(name, [P, cols], dt, offset=base + first * 4)

    x = sb("x", KT * S)
    region("act", 2 * KT * S)
    region("hid", 2 * KT * S)
    region("free", 8320)
    region("kv", 4608)
    region("stats", 3 * S)
    actH = at("actH", ("act", 0), KT * S, F32R)
    actL = at("actL", ("act", KT * S), KT * S, F32R)
    hidH = at("hidH", ("hid", 0), KT * S, F32R)
    hidL = at("hidL", ("hid", KT * S), KT * S, F32R)
    raw = sb("raw", SLOTS * SLAB)
    wH = sb("wH", SLOTS * SLAB, F32R)
    wL = sb("wL", SLOTS * SLAB, F32R)
    const = sb("const", N_CONST)
    cols = sb("cols", 4 * P)
    ones = sb("ones", P)
    one = sb("one", 1)
    gain0 = sb("gain0", KT)
    zero = sb("zero", 1)
    rB = at("rB", ("stats", 0), S)
    acc = at("acc", ("stats", S), S)
    sq = at("sq", ("stats", 2 * S), S)
    rn = sb("rn", ST)
    small = sb("small", 4 * 64)
    modc = sb("modc", 48)
    modx = sb("modx", 16)
    silu_c = sb("silu_c", 16)
    gain1 = sb("gain1", 2 * DH)
    gain2 = sb("gain2", 2 * DH)
    ropeT = sb("ropeT", 4 * ST * DH)
    sink = sb("sink", 2 * NH)
    biasx = sb("biasx", 512)
    kHA = at("kHA", ("kv", 0), NKV * (CTX + S), F32R)
    kHB = at("kHB", ("kv", 1536), NKV * (CTX + S), F32R)
    kL = at("kL", ("free", 8320 - NKV * (CTX + S)), NKV * (CTX + S), F32R)
    vA = at("vA", ("kv", 3072), (CT + ST) * NKV * DH)
    vB = at("vB", ("kv", 3840), (CT + ST) * NKV * DH)
    pool_head = sb("pool_head", 16)
    inv_w = sb("inv_w", len(POOL_WINDOWS))
    k_scale = sb("k_scale", ST * NH)
    ssq = sb("ssq", 64)
    stat = sb("stat", 4 * 32)
    ln_col = sb("ln_col", 2 * KT)
    ln_mean = sb("ln_mean", 4 * ST)

    def cv(name):
        a, w = CONST[name]
        return const[:, a:a + w]

    ident = cv("ident")

    def col(name, n):
        g, first, _ = VEC[name]
        return cols[:, bass.ds(n + (g * P + first), 1)]

    g1 = at("g1", ("free", 0), S)
    sg = at("sg", ("free", S), S)
    ur = at("ur", ("free", 2 * S), S)
    h = at("h", ("free", 3 * S), S)
    xnat = at("xnat", ("hid", 0), ST * D)
    vec_rows = at("vec_rows", ("hid", ST * D), 4 * P)
    mod_raw = at("mod_raw", ("free", 4 * S), 4096)
    mod_acc = at("mod_acc", ("free", 4 * S + 4096), 1024)
    hcH = [at("hcH0", ("kv", 4 * S), 4 * CTX, F32R), at("hcH1", ("free", 12 * S + 9 * P), 4 * CTX, F32R)]
    hcL = [at("hcL0", ("hid", 6 * S), 4 * CTX, F32R), at("hcL1", ("hid", 14 * S), 4 * CTX, F32R)]
    ctx_nat = at("ctx_nat", ("kv", 0), CT * D)
    tA = at("tA", ("free", 0), S)
    tB = at("tB", ("free", S), S)
    u_pool = at("u_pool", ("free", 2 * S), 4 * S)
    work = at("work", ("free", 6 * S), 9 * P)
    v1 = at("v1", ("free", 6 * S + 9 * P), ST * ATT)
    pool_w = at("pool_w", ("free", 10 * S + 9 * P), 4 * P)
    kctx = at("kctx", ("kv", 0), 4 * P)
    rel = at("rel", ("free", 12 * S + 9 * P), 2 * S)
    qiT = at("qiT", ("hid", 0), 2 * S)
    kiT = at("kiT", ("hid", 2 * S), S)
    pi = at("pi", ("hid", KT * S), ST * IDX_COLS)
    q1 = at("q1", ("hid", 0), ST * ATT)
    k1 = at("k1", ("hid", KT * S), ST * ATT)
    qT1 = at("qT1", ("act", 0), 4 * S)
    kT1 = at("kT1", ("act", 4 * S), 4 * S)
    attn1 = at("attn1", ("free", 2 * S), ST * ATT)
    prob1 = at("prob1", ("act", 8 * S), 3 * 768)
    probT1 = at("probT1", ("act", 8 * S + 3 * 768), 2 * 768)
    prob2 = at("prob2", ("free", 8 * S), 3 * 768)
    probT2 = at("probT2", ("stats", 0), 2 * 768)
    nat = at("nat", ("free", 0), ST * 1536)
    bias2 = at("bias2", ("free", ST * 1536), 1536)
    tC = at("tC", ("free", ST * 1536 + 1536), 640)
    gates = at("gates", ("hid", 0), 16 * S)
    qA = at("qA", ("act", 0), NH * S, F32R)
    qB = at("qB", ("act", NH * S), NH * S, F32R)
    attnA = at("attnA", ("free", 0), ST * ATT)
    attnB = at("attnB", ("free", ST * ATT), ST * ATT)
    mA = at("mA", ("free", 2 * ST * ATT), S)
    mB = at("mB", ("free", 2 * ST * ATT + S), S)
    cg = at("cg", ("free", 0), 2 * S)
    cu = at("cu", ("free", 2 * S), 2 * S)
    h3 = at("h3", ("free", 6 * S), S)
    sq2 = at("sq2", ("free", 4 * S), 2 * S)
    dev = at("dev", ("free", 10 * S), 2 * S)
    ln2_gB = at("ln2_gB", ("kv", 0), D)
    ln2_bB = at("ln2_bB", ("kv", D), D)
    out_nat = at("out_nat", ("free", 8 * S), ST * D)

    ps = stack.enter_context(nc.psum_tensor("ps", [P, 8, 512], F32))

    def sem(name):
        return stack.enter_context(nc.semaphore(name))

    x_in = [sem(f"x_in{q}") for q in range(ST)]
    vec_in, const_in, misc_in, ctx_in, bias_in = sem("vec_in"), sem("const_in"), sem("misc_in"), sem("ctx_in"), sem("bias_in")
    tables_in = sem("tables_in")
    raw_in = [sem(f"raw_in{j}") for j in range(SLOTS)]
    mod_in = [sem(f"mod_in{q}") for q in range(2)]
    cleared = sem("cleared")
    hi_ready = sem("hi_ready")
    lo_ready = sem("lo_ready")
    slab_done = sem("slab_done")
    drained_v, drained_a = sem("drained_v"), sem("drained_a")
    v_step, a_step, p_step = sem("v_step"), sem("a_step"), sem("p_step")
    vec_T, cols_ready = sem("vec_T"), sem("cols_ready")
    gain_in, gain_T, gain_ready = sem("gain_in"), sem("gain_T"), sem("gain_ready")
    xT = sem("xT")
    act_hi = sem("act_hi")
    act_ready = sem("act_ready")
    hid_ready = sem("hid_ready")
    sq_ready = sem("sq_ready")
    acc_done = sem("acc_done")
    row_sum, rn_ready, row_bcast = sem("row_sum"), sem("rn_ready"), sem("row_bcast")
    stat_out = sem("stat_out")
    silu_ready = sem("silu_ready")
    silu_c_ready = sem("silu_c_ready")
    mod_half, mod_sum, mod_cols = sem("mod_half"), sem("mod_sum"), sem("mod_cols")
    ctx_T, ctx_drained, hc_ready = sem("ctx_T"), sem("ctx_drained"), sem("hc_ready")
    kctx_ready = sem("kctx_ready")
    idx_rot, idx_T, idx_cols, idx_qk, idx_rel, idx_rel_used = (sem(n) for n in (
        "idx_rot", "idx_T", "idx_cols", "idx_qk", "idx_rel", "idx_rel_used"))
    pooled, pool_mm, pool_hi = sem("pooled"), sem("pool_mm"), sem("pool_hi")
    k_scaled, k_rot = sem("k_scaled"), sem("k_rot")
    qk_sq, qk_rot, qk_T, qk_out = sem("qk_sq"), sem("qk_rot"), sem("qk_T"), sem("qk_out")
    att_qk, q2_rot, q2_T, q2_hi, q2_lo, k2_hi = (sem(n) for n in ("att_qk", "q2_rot", "q2_T", "q2_hi", "q2_lo", "k2_hi"))
    logit, probs, prob_T, probT_a, probT_v, pv, attn_out = (sem(n) for n in (
        "logit", "probs", "prob_T", "probT_a", "probT_v", "pv", "attn_out"))
    at_T, at_hi = sem("at_T"), sem("at_hi")
    sq_summed = sem("sq_summed")
    mean_sum, centred, scaled, shifted = sem("mean_sum"), sem("centred"), sem("scaled"), sem("shifted")
    conv_c = sem("conv_c")
    fin_T, fin_norm, stored = sem("fin_T"), sem("fin_norm"), sem("stored")
    fin_v, fin_p, gb_in = sem("fin_v"), sem("fin_p"), sem("gb_in")

    def units1():
        for tile in reversed(range(ST)):
            for head in range(NH):
                w, off = P * (tile + 1), DH * (head % 2)
                yield dict(W=w,
                           products=[(0, [(qT1[off:off + DH, (head // 2) * S + tile * P:][:, 0:P],
                                           kT1[off:off + DH, (head // 2) * S:(head // 2) * S + w])])], col0=0,
                           mask=cv("causal") if tile == 0 else work[:, P * (tile * (tile + 1) // 2 - 1):][:, 0:w],
                           v=[v1[:, b * ATT + head * DH:][:, 0:DH] for b in range(tile + 1)],
                           out=attn1[:, tile * ATT + head * DH:][:, 0:DH], sink=None)

    def units2(q, kH, high, v, out, banded):
        for tile in range(ST):
            for head in range(NH):
                kv = head // (NH // NKV)
                latents, context = [kv * (CTX + S) + CTX + n * P for n in range(-1, ST)], kv * (CTX + S)
                mask, col0 = zero[:, 0:1].broadcast_to([P, CTX + S]), 0
                if not banded:
                    blocks, pieces = list(range(CT + ST)), [(context, 512), (context + 512, 256)]
                elif tile == 0:
                    blocks, pieces, mask = [2, 3, 0, 1], [(latents[1], 256), (context, 256)], cv("band")[:, P:5 * P]
                elif tile == ST - 1:
                    blocks, pieces, mask = [0, 1, 4, 5], [(context, 256), (latents[tile], 256)], cv("band")[:, 3 * P:]
                else:
                    blocks, mask, col0 = [tile + 1, tile + 2, tile + 3, 0, 1], cv("band")[:, 0:5 * P], P
                    pieces = [(latents[tile - 1], 256), (latents[tile + 1], 256), (context, 256)]
                products, at_col = [], 0
                a = head * S + tile * P
                for key, w in pieces:
                    products.append((at_col, [(q[:, a:a + P], kH[:, key:key + w]),
                                              (q[high, a:a + P], kL[high, key:key + w])]))
                    at_col += w
                yield dict(W=P * len(blocks), products=products, col0=col0, mask=mask,
                           v=[v[:, b * NKV * DH + kv * DH:][:, 0:DH] for b in blocks],
                           out=out[:, tile * ATT + head * DH:][:, 0:DH], sink=head if banded else None)

    lower, upper = slice(0, DH), slice(DH, P)
    group1 = list(units1())
    group2 = list(units2(qA, kHA, lower, vA, attnA, True)) + list(units2(qB, kHB, upper, vB, attnB, False))
    TURNS2 = ([("c", n, 0, 0) for n in range(2)] + [("k", n, kv, 0) for n in range(2) for kv in range(NKV)]
              + [("q", n, h, q) for n in range(2) for q in range(ST) for h in range(2)])
    K_TURNS = 6
    TURN_BANK = [4, 5, 6, 7, 4, 5] + [n % 8 for n in range(K_TURNS, len(TURNS2))]


    ACC_TOTAL = [KT, 2 * KT, 3 * KT, 5 * KT, 6 * KT]
    ACT_BEFORE = {"f1": 0, "f2": 2 * KT, "f3": 5 * KT}
    SILU_BEFORE = {f"f{a}_up{n}": NF * (a - 1) + f0 for a in (1, 2) for n, (f0, _) in enumerate(PARTS)}
    LN_STEPS = (("x", 0), ("x", 1), ("x", 2), ("x", 3), ("c", 0), ("d", 0), ("d", 1), ("s", 0),
                ("x", 4), ("d", 2), ("s", 1), ("d", 3), ("s", 2), ("x", 5), ("d", 4), ("s", 3), ("d", 5), ("s", 4),
                ("x", 6), ("d", 6), ("s", 5), ("u", 7), ("d", 7), ("s", 6), ("a", 7), ("s", 7))
    SQUARES_IN_SLAB = ((0, 1), (2, 3), (4, 5), (6,))
    SUMMED = {k: sum(what in "xas" for what, _ in LN_STEPS[:n + 1]) for n, (s_, k) in enumerate(LN_STEPS) if s_ == "s"}
    BY_POOL = (2, 5)
    BY_V = tuple(n for n in range(2 * ST) if n not in BY_POOL)
    FIN_BANK = (4, 6, 7, 0, 1, 2, 3, 5)
    MISC_DMAS = 7
    wide = [u["W"] > 512 for u in group1 + group2]
    WIDE = [sum(wide[:n]) for n in range(len(wide) + 1)]
    vec_sources = [("ffn1_norm", t["ffn1_norm"][0]), ("mix_norm", t["mix_norm"][0]), ("ffn2_norm", t["ffn2_norm"][0]),
                   ("b_mod", t["b_mod_2"][0]), ("b_gate", t["b_in_2"][0, 1536:]), ("ln1_g", t["ln1_g_2"][0]),
                   ("ln1_b", t["ln1_b_2"][0]), ("ln2_g", t["ln2_g_2"][0]), ("ln2_b", t["ln2_b_2"][0]),
                   ("c", t["c_2"][0]), ("c_ctx", t["c_ctx_2"]), ("pool_scale", t["pool_scale"][0]),
                   ("conv_b", t["conv_b_2"][0]), ("conv_w0", t["conv_w_2"][0, 0]), ("conv_w1", t["conv_w_2"][0, 1]),
                   ("conv_w2", t["conv_w_2"][0, 2])]
    VEC_DMAS = len(vec_sources) - 1

    def tile(buf, n, w=S):
        return buf[:, bass.ds(n * w, w)]

    def bank(b, w=512, first=0):
        return ps[:, b, first:first + w]

    def turned(n):
        what, branch, h, q = TURNS2[n]
        own, other = (lower, upper) if branch == 0 else (upper, lower)
        src = ps[own, TURN_BANK[n], :].rearrange("p (m s) -> p m s", m=2 if what == "c" else 4)
        if what == "q":
            into = (qA, qB)[branch][:].rearrange("p (m s) -> p m s", m=NH)[:, 4 * h:4 * h + 4, q * P:(q + 1) * P]
            return src, into[own], into[other], None
        high, low = ((b[:].rearrange("p (v s) -> p v s", v=NKV)) for b in ((kHA, kHB)[branch], kL))
        if what == "c":
            return src, high[own, :, 0:CTX], low[own, :, 0:CTX], high[other, :, 0:CTX]
        src = ps[own, TURN_BANK[n], :]
        return src, high[own, h, CTX:], low[own, h, CTX:], high[other, h, CTX:]

    def out_block(n):
        return out_nat[:, (n % ST) * D + (n // ST) * 512:][:, 0:512]

    block = stack.enter_context(nc.Block())

    def rotate(E, link, v, tmp, heads, groups, half, cos, sin, last=None):
        w = groups * 2 * half
        x5 = v if groups == 1 else v.rearrange("p h (g r) -> p h g r", g=groups)
        t5 = tmp if groups == 1 else tmp.rearrange("p h (g r) -> p h g r", g=groups)
        s5 = sin if groups == 1 else sin.rearrange("p (g r) -> p g r", g=groups)
        for to, frm in ((0, half), (half, 0)):
            if groups == 1:
                link(E.tensor_tensor(t5[:, :, to:to + half], x5[:, :, frm:frm + half],
                                     s5[:, to:to + half].unsqueeze(1).broadcast_to([P, heads, half]), ALU.mult))
            else:
                link(E.tensor_tensor(t5[:, :, :, to:to + half], x5[:, :, :, frm:frm + half],
                                     s5[:, :, to:to + half].unsqueeze(1).broadcast_to([P, heads, groups, half]),
                                     ALU.mult))
        link(E.tensor_tensor(v, v, cos.unsqueeze(1).broadcast_to([P, heads, w]), ALU.mult))
        ins = E.tensor_tensor(v, v, tmp, ALU.add)
        if last is None:
            link(ins)
        else:
            ins.then_inc(last, 1)

    def gained(n, part, q):
        return ropeT[:, (2 * n + part) * ST * DH + q * DH:][:, 0:DH]

    def heads_rotated(E, chain, src, n, tmp, scales, done):
        link = chain.link
        for q in range(ST):
            v = src[:, q * ATT:(q + 1) * ATT].rearrange("p (h d) -> p h d", h=NH)
            link(E.tensor_tensor(v, v, scales[:, q * NH:][:, 0:NH].unsqueeze(2).broadcast_to([P, NH, DH]), ALU.mult))
            rotate(E, link, v, tmp[:].rearrange("p (h d) -> p h d", h=NH), NH, 1, DH // 2,
                   gained(n, 0, q), gained(n, 1, q), last=done)
            chain.engine.wait_ge(done, q + 1)

    @block.sync
    def _(sp):
        for q in range(ST):
            sp.dma_start(xnat[:, q * D:(q + 1) * D], t["x"][0, q * P:(q + 1) * P, :]).then_inc(x_in[q], 16)

        def slab(st, i, j, first=False):
            if not first:
                sp.wait_ge(lo_ready, i * 4 + (st["base"] + j - 3))
            for c, src in st["sources"](i, j):
                k, n = src.shape[1], src.shape[2]
                dst = raw[:, j * SLAB + c * P:j * SLAB + c * P + k * n].rearrange("p (k n) -> p k n", k=k)
                sp.dma_start(dst, src).then_inc(raw_in[j], 16)

        def slabs(st, first, end):
            def body(i):
                for j in range(SLOTS):
                    slab(st, i, j)
            loop(sp, first, end, body)

        for st in stages:
            begun = 0
            if st["name"] == "f1_up0":
                for j in range(SLOTS):
                    slab(st, 0, j, first=True)
                begun = 1
            if st["name"] == "k":
                sp.wait_ge(mod_cols, 12)
                sp.dma_start(pool_w[:].rearrange("c (g d) -> c g d", g=4),
                             t["pool_w"][0].rearrange("g c d -> c g d")).then_inc(misc_in, 16)
            if st["name"] == "f2_up1":
                sp.wait_ge(slab_done, stage_of["f2_up0"]["base"])
                sp.dma_start(bias2[:], t["b_in_2"][0:1, 0:1536].broadcast_to([P, 1536])).then_inc(bias_in, 16)
            if st["name"] == "f3_up1":
                sp.wait_ge(slab_done, stage_of["f3_up0"]["base"])
                sp.dma_start(ln2_gB[:], t["ln2_g_2"].broadcast_to([P, D])).then_inc(gb_in, 16)
                sp.dma_start(ln2_bB[:], t["ln2_b_2"].broadcast_to([P, D])).then_inc(gb_in, 16)
            slabs(st, begun, st["its"])
        for n in range(2 * ST):
            half, q = n // ST, n % ST
            if n in BY_POOL:
                sp.wait_ge(fin_p, BY_POOL.index(n) + 1)
            else:
                sp.wait_ge(fin_v, BY_V.index(n) + 1)
            sp.dma_start(t["out"][0, q * P:(q + 1) * P, half * 512:(half + 1) * 512],
                         out_nat[:, q * D + half * 512:q * D + half * 512 + 512]).then_inc(stored, 16)
        sp.wait_ge(stored, 16 * 2 * ST)

    @block.gpsimd
    def _(pool):
        nc.gpsimd.memset(vec_rows[:], 0.0).then_inc(cleared, 1)
        nc.gpsimd.memset(ones[:], 1.0 / D).then_inc(cleared, 1)
        nc.gpsimd.memset(one[:], 1.0).then_inc(cleared, 1)
        nc.gpsimd.memset(zero[:], 0.0).then_inc(cleared, 1)
        for g, w in enumerate(POOL_WINDOWS):
            nc.gpsimd.memset(inv_w[:, g:g + 1], 1.0 / w).then_inc(cleared, 1)

        def lows(st, i, then=None):
            for j in range(SLOTS):
                a, w = j * SLAB, st["width"]
                pool.wait_ge(hi_ready, i * 4 + (st["base"] + j + 1))
                nc.gpsimd.tensor_tensor(wL[:, a:a + w], raw[:, a:a + w], wH[:, a:a + w].bitcast(F32),
                                        ALU.subtract).then_inc(lo_ready, 1)
                if then:
                    then(j)

        chain = Chain(pool, p_step)
        link = chain.link
        G = nc.gpsimd

        def pooling(g):
            u, w = tile(u_pool, g), POOL_WINDOWS[g]
            pool.wait_ge(drained_a, drain_base["pool"] + g + 1)
            pool.wait_ge(stat_out, 2)
            pool.wait_ge(tables_in, 16)
            link(G.tensor_tensor(u, u, rB[:], ALU.mult))
            src, step, bufs = u, 1, [tB, sq]
            while step < w:
                dst = bufs[0][:]
                bufs = bufs[::-1]
                G.tensor_tensor(dst[:, step:], src[:, step:], src[:, 0:S - step], ALU.add)
                link(G.tensor_copy(dst[:, 0:step], src[:, 0:step]))
                src, step = dst, 2 * step
            head = pool_head[:, 0:w - 1]
            link(G.tensor_tensor(head, src[:, 0:w - 1], cv("inv_count")[:, 0:w - 1], ALU.mult))
            link(G.tensor_tensor(head, head, u[:, 0:w - 1], ALU.subtract))
            link(G.tensor_tensor(src, src, inv_w[:, g:g + 1].broadcast_to([P, S]), ALU.mult))
            link(G.tensor_tensor(u, src, u, ALU.subtract))
            G.tensor_copy(u[:, 0:w - 1], head).then_inc(pooled, 1)
            pool.wait_ge(pooled, g + 1)

        for st in stages:
            if st["name"] == "q":
                lows(st, 0, then=pooling)
            elif st["name"] == "out1":
                pool.wait_ge(k_scaled, 1)
                heads_rotated(G, chain, k1, 1, sq, k_scale[:], k_rot)
                loop(pool, 0, st["its"], lambda i, st=st: lows(st, i))
            else:
                loop(pool, 0, st["its"], lambda i, st=st: lows(st, i))
        for k in range(KT):
            pool.wait_ge(sq_ready, 4 * KT + k + 1)
            if k == 0:
                pool.wait_ge(rn_ready, 4)
                G.tensor_copy(sq[:], tile(sq2, 0)).then_inc(sq_summed, 1)
            else:
                G.tensor_tensor(sq[:], sq[:], tile(sq2, k % 2), ALU.add).then_inc(sq_summed, 1)
            pool.wait_ge(sq_summed, k + 1)
        for n in BY_POOL:
            o, half = out_block(n), n // ST
            pool.wait_ge(fin_norm, n + 1)
            pool.wait_ge(gb_in, 32)
            link(G.tensor_tensor(o, o, ln2_gB[:, half * 512:half * 512 + 512], ALU.mult))
            G.tensor_tensor(o, o, ln2_bB[:, half * 512:half * 512 + 512], ALU.add).then_inc(fin_p, 1)

    @block.tensor
    def _(pe):
        def product(out, a, b, first, last):
            return nc.tensor.matmul(out, a, b, start=first, stop=last)

        def split_product(out, wh, wl, xh, xl, first, last):
            product(out, wh, xh, first, False)
            product(out, wh, xl, False, False)
            return product(out, wl, xh, False, last)

        def row_sums(n):
            pe.wait_ge(acc_done, ACC_TOTAL[n])
            for q in range(ST):
                mm = product(ps[:, 4, q:q + 1], acc[:, q * P:(q + 1) * P], ones[:, 0:1], True, True)
            mm.then_inc(row_sum, 1)

        def spread_rows(n):
            pe.wait_ge(rn_ready, n + 1)
            for q in range(ST):
                mm = product(bank(5, P, q * P), rn[:, q:q + 1].broadcast_to([P, P]), ident, True, True)
            mm.then_inc(row_bcast, 1)

        def feature_tiles(name, opH, opL, ready, K=KT, drained=drained_v, after=None, late=None, peel=0, during=None, tail=None):
            """Slabs of a feature tile each: out[feature, token] += w[k, feature] op[k, token]."""
            st = stage_of[name]

            def body(i):
                for j in range(SLOTS):
                    pe.wait_ge(lo_ready, i * 4 + (st["base"] + j + 1))
                    pe.wait_ge(drained, i * 4 + (drain_base[name] + j - 3))
                    for k in range(K):
                        if j == 0:
                            pe.wait_ge(ready[0], ready[1] + k + 1)
                        a = j * SLAB + k * P
                        mm = split_product(bank(j), wH[:, a:a + P], wL[:, a:a + P],
                                           opH[:, k * S:(k + 1) * S], opL[:, k * S:(k + 1) * S], k == 0, k == K - 1)
                        if during and (i, j, k) == (1, 0, 3):
                            during()
                    mm.then_inc(slab_done, 1)
                    if after and isinstance(i, int):
                        after(i, j)
                    if tail and isinstance(i, int):
                        tail(j)
                    if late and j == 1 and not (isinstance(i, int) and i == 0):
                        late(i - 1)
            for i in range(peel):
                body(i)
            loop(pe, peel, st["its"] - (1 if tail else 0), body)
            if tail:
                body(st["its"] - 1)

        def token_tiles(name, width, bank0, before, after=None):
            st = stage_of[name]
            before()
            for j in range(SLOTS):
                pe.wait_ge(lo_ready, st["base"] + j + 1)
                for kk in range(2):
                    k, a = 2 * j + kk, j * SLAB + kk * width
                    for q in range(ST):
                        xh, xl = (b[:, k * S + q * P:k * S + (q + 1) * P] for b in (actH, actL))
                        o = bank(bank0 + q, width)
                        product(o, xh, wH[:, a:a + width], k == 0, False)
                        product(o, xl, wH[:, a:a + width], False, False)
                        mm = product(o, xh, wL[:, a:a + width], False, k == KT - 1)
                mm.then_inc(slab_done, 1)
                if after:
                    after(j)

        def vector_turns():
            pe.wait_ge(vec_in, VEC_DMAS * 16)
            pe.wait_ge(gain_ready, 1)
            for g in range(4):
                mm = nc.tensor.transpose(bank(7, P, g * P), vec_rows[:, g * P:(g + 1) * P], ident)
            mm.then_inc(vec_T, 1)

        pe.wait_ge(const_in, 16)
        for k in range(KT):
            if k >= 4:
                pe.wait_ge(drained_v, k - 3)
            for q in range(ST):
                if k == 0:
                    pe.wait_ge(x_in[q], 16)
                mm = nc.tensor.transpose(bank(k % 4, P, q * P), xnat[:, q * D + k * P:q * D + (k + 1) * P], ident)
            mm.then_inc(xT, 1)
            if k == 0:
                pe.wait_ge(gain_in, 16)
                nc.tensor.transpose(bank(7, KT), vec_rows[0:KT, 0:P], ident[0:KT, 0:KT]).then_inc(gain_T, 1)
        vector_turns()

        def up_down(name, hid0, first_hook, sums=None, during=None):
            for n, (f0, nf) in enumerate(PARTS):
                hooked = first_hook if n == 0 else None
                if name == "f1" and n == 2:
                    context_turn()
                feature_tiles(f"{name}_up{n}", actH, actL, (act_ready, ACT_BEFORE[name]), after=hooked,
                              peel=1 if n == 0 or sums else 0,
                              late=(lambda i, n=n: sums(n, i)) if sums else None)
                feature_tiles(f"{name}_down{n}", hidH, hidL, (hid_ready, hid0 + f0), K=nf,
                              after=(lambda i, j, n=n, nf=nf: (i, j) == (0, 1) and sums(n, nf // 2 - 1)) if sums else None,
                              during=during if n == 2 else None, peel=1 if sums or during and n == 2 else 0)

        def norm_hook(n):
            def after(i, j):
                if (i, j) == (0, 0):
                    row_sums(n)
                if (i, j) == (0, 1):
                    spread_rows(n)
            return after

        def mod_sums(i, ctx_too):
            pe.wait_ge(mod_half, (i + 1) * 2)
            if not isinstance(i, int) or i > 0:
                pe.wait_ge(mod_cols, i)
            for q in range(8 if ctx_too else 4):
                mm = product(ps[:, 6, q:q + 1], mod_acc[:, q * P:(q + 1) * P], one[:, 0:1], True, True)
            mm.then_inc(mod_sum, 1)

        def context_turn():
            pe.wait_ge(ctx_in, 16)
            pe.wait_ge(mod_cols, 8)
            pe.wait_ge(stat_out, 1)
            pe.wait_ge(cols_ready, 1)
            for k in range(KT):
                for q in range(CT):
                    mm = nc.tensor.transpose(bank(4 + k // 2, P, (k % 2) * CTX + q * P),
                                             ctx_nat[:, q * D + k * P:q * D + (k + 1) * P], ident)
            mm.then_inc(ctx_T, 1)

        def f1_sums(n, i):
            if n == 2 and isinstance(i, int) and i == 0:
                pe.wait_ge(ctx_drained, KT)
            mod_sums(i + n * 4, n == 0)

        up_down("f1", 0, norm_hook(0), f1_sums)
        mod_sums(11, False)

        st = stage_of["ctxkv"]
        for j in range(SLOTS):
            pe.wait_ge(lo_ready, st["base"] + j + 1)
            for kk in range(4):
                k, a = 4 * (j % 2) + kk, j * SLAB + kk * 256
                pe.wait_ge(hc_ready, k + 1)
                at_k = (k % 4) * CTX
                for q in range(CT):
                    b = 2 * (j // 2) + q
                    if k == 0:
                        pe.wait_ge(drained_v, drain_base["ctxkv"] - 3 + b)
                    xh, xl = (c[k // 4][:, at_k + q * P:at_k + (q + 1) * P] for c in (hcH, hcL))
                    product(bank(b, 256), xh, wH[:, a:a + 256], k == 0, False)
                    product(bank(b, 256), xl, wH[:, a:a + 256], False, False)
                    mm = product(bank(b, 256), xh, wL[:, a:a + 256], False, k == KT - 1)
            mm.then_inc(slab_done, 1)
            if j == 0:
                row_sums(1)
            if j == 2:
                spread_rows(1)

        def before_idx():
            pe.wait_ge(act_ready, 2 * KT)
            pe.wait_ge(stat_out, 2)
            pe.wait_ge(mod_cols, 12)

        token_tiles("idx", IDX_COLS, 4, before_idx)

        def idx_turns():
            pe.wait_ge(idx_rot, ST)
            for q in range(ST):
                a = q * IDX_COLS
                for pair in range(2):
                    nc.tensor.transpose(bank(4 + pair, P, q * P), pi[:, a + pair * P:a + (pair + 1) * P], ident)
                mm = nc.tensor.transpose(ps[0:IDX_DIM, 6, q * P:(q + 1) * P], pi[:, a + 2 * P:a + 2 * P + IDX_DIM], ident)
            mm.then_inc(idx_T, 1)

        def idx_scores():
            pe.wait_ge(idx_cols, 4)
            for n in range((ST - 1) * IDX_HEADS):
                q, head = n // IDX_HEADS + 1, n % IDX_HEADS
                off = IDX_DIM * (head % 2)
                if n >= 4:
                    pe.wait_ge(idx_rel, n - 3)
                product(bank(4 + n % 4, P * (q + 1)), qiT[off:off + IDX_DIM, (head // 2) * S + q * P:][:, 0:P],
                        kiT[off:off + IDX_DIM, 0:P * (q + 1)], True, True).then_inc(idx_qk, 1)

        st = stage_of["pool"]
        for j in range(SLOTS):
            pe.wait_ge(lo_ready, st["base"] + j + 1)
            pe.wait_ge(drained_v, drain_base["ctxkv"] + j + 1)
            for k in range(KT):
                a = j * SLAB + k * P
                mm = split_product(bank(j), wH[:, a:a + P], wL[:, a:a + P], actH[:, k * S:(k + 1) * S],
                                   actL[:, k * S:(k + 1) * S], k == 0, k == KT - 1)
            mm.then_inc(slab_done, 1)
            if j == 1:
                idx_turns()
        idx_scores()
        token_tiles("q", ATT, 4, lambda: pe.wait_ge(idx_rel, 12))
        token_tiles("k", ATT, 0, lambda: pe.wait_ge(drained_a, drain_base["pool"] + 4))
        token_tiles("v", ATT, 4, lambda: pe.wait_ge(drained_a, drain_base["q"] + 4))

        pe.wait_ge(drained_a, drain_base["k"] + 4)
        pe.wait_ge(pooled, 4)
        pe.wait_ge(misc_in, MISC_DMAS * 16 + 16)
        pe.wait_ge(drained_a, drain_base["v"] + 4)
        for g in range(4):
            product(bank(4 + g), pool_w[:, g * P:(g + 1) * P], u_pool[:, g * S:(g + 1) * S], True, True).then_inc(pool_mm, 1)
        for n in range(2 * ST):
            src, q = (q1, k1)[n // ST], n % ST
            pe.wait_ge((qk_rot, k_rot)[n // ST], q + 1)
            if n >= 4:
                pe.wait_ge(qk_out, n - 3)
            for pair in range(4):
                mm = nc.tensor.transpose(bank(n % 4, P, pair * P), src[:, q * ATT + pair * P:][:, 0:P], ident)
            mm.then_inc(qk_T, 1)

        pe.wait_ge(tables_in, 16)
        def warm(n):
            for _ in range(n):
                product(bank(5), ident, const[:, 0:512], True, True)

        def attention(units, n0, prob, probT):
            def logits(n):
                u = units[n - n0]
                if n - n0 >= 2:
                    pe.wait_ge(logit, n - 1)
                b = 2 * (n % 2)
                for c, pairs in u["products"]:
                    for m, (q, keys) in enumerate(pairs):
                        mm = product(bank(b + c // 512, keys.shape[1], c % 512), q, keys, m == 0, m == len(pairs) - 1)
                mm.then_inc(att_qk, 1)

            def turn(n):
                u = units[n - n0]
                pe.wait_ge(probs, n + 1)
                if n > 0:
                    pe.wait_ge(probT_a, n)
                if n > n0 and units[n - 1 - n0]["W"] > 512:
                    pe.wait_ge(probT_v, WIDE[n])
                for b in range(u["W"] // P):
                    mm = nc.tensor.transpose(bank(4 + b // 4, P, (b % 4) * P),
                                             prob[:, (n % 3) * 768 + b * P:][:, 0:P], ident)
                mm.then_inc(prob_T, 1)

            def values(n):
                u = units[n - n0]
                pe.wait_ge(probT_a, n + 1)
                if u["W"] > 512:
                    pe.wait_ge(probT_v, WIDE[n + 1])
                if n >= 2:
                    pe.wait_ge(attn_out, n - 1)
                for b, v in enumerate(u["v"]):
                    mm = product(bank(6 + n % 2, DH), probT[:, (n % 2) * 768 + b * P:][:, 0:P], v,
                                 b == 0, b == len(u["v"]) - 1)
                mm.then_inc(pv, 1)

            end = n0 + len(units)
            logits(n0)
            logits(n0 + 1)
            warm(5)
            for n in range(n0, end):
                turn(n)
                if n + 2 < end:
                    logits(n + 2)
                if n > n0:
                    values(n - 1)
            values(end - 1)

        pe.wait_ge(qk_out, 8)
        pe.wait_ge(drained_a, drain_base["v"] + 4)
        pe.wait_ge(hid_ready, NF + 4)
        attention(group1, 0, prob1, probT1)
        pe.wait_ge(attn_out, len(group1))
        for k in range(4):
            for q in range(ST):
                mm = nc.tensor.transpose(bank(k, P, q * P), attn1[:, q * ATT + k * P:][:, 0:P], ident)
            mm.then_inc(at_T, 1)
        pe.wait_ge(hid_ready, NF + KT)
        feature_tiles("out1", hidH, hidL, (hid_ready, NF))

        up_down("f2", NF + KT, norm_hook(2))

        def before_proj0():
            pe.wait_ge(act_ready, 4 * KT)
            pe.wait_ge(stat_out, 3)

        token_tiles("proj0", 512, 4, before_proj0)
        token_tiles("proj1", 512, 0, lambda: pe.wait_ge(drained_v, drain_base["proj0"]))
        token_tiles("proj2", 512, 4, lambda: pe.wait_ge(drained_v, drain_base["proj1"]))
        pe.wait_ge(drained_v, drain_base["proj2"])
        def turn2(n):
            what, branch, h, q = TURNS2[n]
            before = [m for m in range(n) if TURN_BANK[m] == TURN_BANK[n]]
            if before:
                pe.wait_ge(q2_lo, before[-1] + 1)
            elif n >= K_TURNS:
                pe.wait_ge(drained_a, drain_base["gates"] + 16)
            if what == "q":
                src = [nat[:, q * 1536 + branch * 768 + (4 * h + m) * DH - branch * DH:] for m in range(4)]
            elif what == "k":
                src = [nat[:, m * 1536 + branch * 768 + ATT + h * DH - branch * DH:] for m in range(ST)]
            else:
                src = [kctx[:, (2 * branch + m % 2) * P + (m // 2) * DH - branch * DH:] for m in range(4)]
            rows = DH * (branch + 1)
            for m in range(4):
                mm = nc.tensor.transpose(ps[0:rows, TURN_BANK[n], m * P:(m + 1) * P], src[m][:, 0:rows], ident)
            mm.then_inc(q2_T, 1)

        def key_turns(j):
            if j == 0:
                pe.wait_ge(drained_v, drain_base["merge"])
                pe.wait_ge(q2_rot, 1)
                pe.wait_ge(kctx_ready, 2)
                for n in range(4):
                    turn2(n)
            if j == 3:
                for n in range(4, K_TURNS):
                    turn2(n)

        pe.wait_ge(drained_v, drain_base["proj2"])
        feature_tiles("gates", actH, actL, (act_ready, 3 * KT), drained=drained_a, tail=key_turns)
        for n in range(K_TURNS, len(TURNS2)):
            turn2(n)
        pe.wait_ge(q2_lo, len(TURNS2))
        attention(group2, len(group1), prob2, probT2)
        pe.wait_ge(attn_out, len(group1) + len(group2))
        for k in range(KT):
            src = attnA if k < 4 else attnB
            for q in range(ST):
                mm = nc.tensor.transpose(bank(k, P, q * P), src[:, q * ATT + (k % 4) * P:][:, 0:P], ident)
            mm.then_inc(at_T, 1)

        def merge(i):
            for j in range(SLOTS):
                pe.wait_ge(lo_ready, i * 4 + (stage_of["merge"]["base"] + j + 1))
                pe.wait_ge(drained_v, i * 4 + (drain_base["merge"] + j - 3))
                for k in range(KT):
                    if j == 0:
                        pe.wait_ge(act_ready, 4 * KT + KT)
                    a = j * SLAB + k * P
                    mm = split_product(bank(j + 4 * (k // 4)), wH[:, a:a + P], wL[:, a:a + P],
                                       actH[:, k * S:(k + 1) * S], actL[:, k * S:(k + 1) * S], k % 4 == 0, k % 4 == 3)
                mm.then_inc(slab_done, 1)
        loop(pe, 0, 2, merge)
        def provisional_mean(n):
            def during():
                pe.wait_ge(acc_done, ACC_TOTAL[2 + n] + 4)
                pe.wait_ge(drained_v, drain_base[("out2", "f3_down2")[n]])
                product(bank(4), ones[:], acc[:], True, True)
                for q in range(ST):
                    mm = product(ps[:, 5, 8 + q:9 + q], acc[:, q * P:(q + 1) * P], ones[:, 0:1], True, True)
                mm.then_inc(mean_sum, 1)
            return during

        def moments(n):
            pe.wait_ge(acc_done, ACC_TOTAL[3 + n])
            if n == 1:
                pe.wait_ge(sq_summed, KT)
            for q in range(ST):
                product(ps[:, 5, q:q + 1], acc[:, q * P:(q + 1) * P], ones[:, 0:1], True, True)
                mm = product(ps[:, 5, 4 + q:5 + q], sq[:, q * P:(q + 1) * P], ones[:, 0:1], True, True)
            mm.then_inc(row_sum, 1)

        feature_tiles("out2", hidH, hidL, (hid_ready, 2 * (NF + KT) - KT), peel=1, during=provisional_mean(0))
        moments(0)
        pe.wait_ge(rn_ready, 4)
        for q in range(ST):
            product(bank(6, P, q * P), rn[:, q:q + 1].broadcast_to([P, P]), ident, True, True)
            mm = product(bank(7, P, q * P), ln_mean[:, q:q + 1].broadcast_to([P, P]), ident, True, True)
        mm.then_inc(row_bcast, 1)
        up_down("f3", 2 * (NF + KT), None, during=provisional_mean(1))

        for n in range(2 * ST):
            half, q = n // ST, n % ST
            if n == 0:
                pe.wait_ge(centred, KT + 1)
                pe.wait_ge(drained_v, drain_base["f3_down2"] + 5)
            if n == ST:
                moments(1)
                pe.wait_ge(drained_v, drain_base["f3_down2"] + KT)
            if n == 2 * ST - 1:
                pe.wait_ge(rn_ready, 5)
            for k in range(4):
                mm = nc.tensor.transpose(bank(FIN_BANK[n], P, k * P), x[:, (4 * half + k) * S + q * P:][:, 0:P], ident)
            mm.then_inc(fin_T, 1)

    @block.scalar
    def _(act):
        chain = Chain(act, a_step)
        link = chain.link
        act.dma_start(ident, t["const"][:, 0:P]).then_inc(const_in, 16)
        act.wait_ge(cleared, 1)
        for name, src in vec_sources:
            g, first, n = VEC[name]
            act.dma_start(vec_rows[first:first + n, g * P:(g + 1) * P],
                          src.rearrange("(r c) -> r c", c=P)).then_inc(gain_in if name == "ffn1_norm" else vec_in, 16)

        def load_mod(chunk, first=False):
            for half in range(2):
                if not first:
                    act.wait_ge(mod_half, chunk * 2 + (half - 1))
                act.dma_start(mod_raw[:, half * 2048:(half + 1) * 2048].rearrange("p (k n) -> p k n", k=4),
                              kview(t["w_mod_2"][0])[:, 4 * half:4 * half + 4, bass.ds(chunk * 512, 512)]
                              ).then_inc(mod_in[half], 16)

        def split(st, i, j):
            if st is None:
                return
            a, w = j * SLAB, st["width"]
            act.wait_ge(raw_in[j], i * (16 * st["dmas"]) + 16 * (st["raw"] + st["dmas"]))
            if st["name"] != "f1_up0" or not isinstance(i, int):
                act.wait_ge(slab_done, i * 4 + (st["base"] + j - 3))
            nc.scalar.activation(wH[:, a:a + w], raw[:, a:a + w], ACT.Copy).then_inc(hi_ready, 1)

        def slabs(name, per, drain, finish=None):
            st = stage_of[name]

            def body(i, then, k):
                for j in range(SLOTS):
                    drain(i, j)
                    split(then, k, j)
                if finish:
                    finish(i)
            chain.loop(0, st["its"] - 1, per, lambda i: body(i, st, i + 1))
            links = chain.links
            body(st["its"] - 1, nxt.get(name), 0)
            assert chain.links - links == per

        act.wait_ge(gain_T, 1)
        nc.scalar.activation(gain0[:], bank(7, KT), ACT.Copy).then_inc(gain_ready, 1)
        act.wait_ge(gain_ready, 1)
        for k in range(KT):
            act.wait_ge(drained_v, k + 1)
            nc.scalar.activation(tile(actH, k), tile(x, k), ACT.Copy, scale=gain0[:, k:k + 1]).then_inc(act_hi, 1)
            if k >= 2:
                act.wait_ge(acc_done, k - 1)
            nc.scalar.activation((sq, rB)[k % 2][:], tile(x, k), ACT.Square).then_inc(sq_ready, 1)
            if k % 2:
                split(stage_of["f1_up0"], 0, k // 2)
            if k == 3:
                load_mod(0, first=True)
        act.dma_start(const[:, P:], t["const"][:, P:]).then_inc(tables_in, 16)
        for dst, src in ((gain1[:, 0:DH], t["q_norm"]), (gain1[:, DH:], t["k_norm"]),
                         (gain2[:, 0:DH], t["q_norm_g_2"]), (gain2[:, DH:], t["k_norm_g_2"]),
                         (sink[:, 0:NH], t["attn_sink_2"]),
                         (biasx[:, 0:256], t["b_in_2"][:, 512:768]), (biasx[:, 256:512], t["b_in_2"][:, 1280:1536])):
            act.dma_start(dst, src.broadcast_to([P, src.shape[1]])).then_inc(misc_in, 16)
        act.dma_start(ctx_nat[:].rearrange("p (q d) -> p q d", q=CT),
                      t["ctx_2"][0].rearrange("(q p) d -> p q d", p=P)).then_inc(ctx_in, 16)
        act.wait_ge(cols_ready, 1)
        for n, name in enumerate(("c", "c_ctx")):
            nc.scalar.activation(silu_c[:, 8 * n:8 * n + 8], cols[:, VEC[name][0] * P + VEC[name][1]:][:, 0:8],
                                 ACT.Silu).then_inc(silu_c_ready, 1)

        def nothing(i, j):
            pass

        def silu(name):
            def drain(i, j):
                if j % 2 == 0:
                    act.wait_ge(drained_v, i * 4 + (drain_base[name] + j + 1))
                    nc.scalar.activation(sg[:], g1[:], ACT.Silu).then_inc(silu_ready, 1)
            return drain

        def normed(name, gain, acc0):
            def drain(i, j):
                m = i * 4 + j
                act.wait_ge(drained_v, i * 4 + (drain_base[name] + j + 1))
                nc.scalar.activation(tile(actH, m), tile(x, m), ACT.Copy, scale=col(gain, m)).then_inc(act_hi, 1)
                act.wait_ge(acc_done, i * 4 + (acc0 + j))
                nc.scalar.activation(sq[:], tile(x, m), ACT.Square).then_inc(sq_ready, 1)
            return drain

        for n in range(len(PARTS)):
            slabs(f"f1_up{n}", 0, silu(f"f1_up{n}"), lambda i, n=n: load_mod(i + (4 * n + 1)))
            slabs(f"f1_down{n}", 0, nothing if n < 2 else normed("f1_down2", "mix_norm", ACC_TOTAL[0]))
        slabs("ctxkv", 0, nothing)

        def token_stage(name, bank0, into, width, wait=None):
            st = stage_of[name]
            for j in range(SLOTS - 1):
                split(nxt[name], 0, j)
            act.wait_ge(slab_done, st["base"] + SLOTS)
            act.wait_ge(rn_ready, 2)
            if wait:
                act.wait_ge(*wait)
            for q in range(ST):
                nc.scalar.activation(into[:, q * width:(q + 1) * width], bank(bank0 + q, width), ACT.Copy,
                                     scale=rn[:, q:q + 1]).then_inc(drained_a, 1)
            split(nxt[name], 0, SLOTS - 1)

        def head_squares(src, n):
            act.wait_ge(drained_a, drain_base[("q", "k")[n]] + 4)
            for q in range(ST):
                for head in range(NH):
                    a = head * DH
                    ins = nc.scalar.activation(rel[:, (q % 2) * S + a:][:, 0:DH], src[:, q * ATT + a:][:, 0:DH],
                                               ACT.Square, accum_out=ssq[:, n * 32 + q * NH + head:][:, 0:1])
                    if head < NH - 1:
                        continue
                    if q < ST - 1:
                        link(ins)
                    else:
                        ins.then_inc(qk_sq, 1)
                        act.wait_ge(qk_sq, n + 1)

        token_stage("idx", 4, pi, IDX_COLS)

        for j in range(SLOTS):
            act.wait_ge(slab_done, stage_of["pool"]["base"] + j + 1)
            nc.scalar.activation(tile(u_pool, j), bank(j), ACT.Copy).then_inc(drained_a, 1)
            split(stage_of["q"], 0, j)
        for n in range((ST - 1) * IDX_HEADS):
            w = P * (n // IDX_HEADS + 2)
            act.wait_ge(idx_qk, n + 1)
            if n >= 2:
                act.wait_ge(idx_rel_used, n - 1)
            nc.scalar.activation(rel[:, (n % 2) * S:][:, 0:w], bank(4 + n % 4, w), ACT.Relu).then_inc(idx_rel, 1)
        token_stage("q", 4, q1, ATT)
        act.wait_ge(idx_rel_used, 12)
        head_squares(q1, 0)
        token_stage("k", 0, k1, ATT)
        head_squares(k1, 1)
        token_stage("v", 4, v1, ATT)

        for g in range(4):
            act.wait_ge(pool_mm, g + 1)
            nc.scalar.activation(tile(hidH, 4 + g), bank(4 + g), ACT.Copy, scale=col("pool_scale", g)).then_inc(pool_hi, 1)
        for n in range(2 * ST):
            into, q = (qT1, kT1)[n // ST], n % ST
            act.wait_ge(qk_T, n + 1)
            nc.scalar.activation(into[:].rearrange("p (a s) -> p a s", a=4)[:, :, q * P:(q + 1) * P],
                                 bank(n % 4).rearrange("p (a s) -> p a s", a=4), ACT.Copy).then_inc(qk_out, 1)

        def attention(units, n0, prob, probT):
            def exps(n):
                u = units[n - n0]
                act.wait_ge(logit, n + 1)
                c = n % 32
                if u["sink"] is not None:
                    link(nc.scalar.activation(stat[:, 64 + c:65 + c], stat[:, c:c + 1], ACT.Exp,
                                              bias=sink[:, u["sink"]:u["sink"] + 1]))
                p = prob[:, (n % 3) * 768:][:, 0:u["W"]]
                nc.scalar.activation(p, p, ACT.Exp, scale=-1.0, bias=stat[:, c:c + 1],
                                     accum_out=stat[:, 32 + c:33 + c]).then_inc(probs, 1)

            def copy(n):
                u = units[n - n0]
                w = min(512, u["W"])
                act.wait_ge(prob_T, n + 1)
                if n >= 2:
                    act.wait_ge(pv, n - 1)
                nc.scalar.activation(probT[:, (n % 2) * 768:][:, 0:w], bank(4, w), ACT.Copy).then_inc(probT_a, 1)

            end = n0 + len(units)
            exps(n0)
            for n in range(n0, end):
                if n + 1 < end:
                    exps(n + 1)
                copy(n)

        attention(group1, 0, prob1, probT1)
        for k in range(4):
            act.wait_ge(at_T, k + 1)
            nc.scalar.activation(tile(hidH, k), bank(k), ACT.Copy).then_inc(at_hi, 1)

        slabs("out1", 0, normed("out1", "ffn2_norm", ACC_TOTAL[1]))

        def modulated(i, j):
            m = i * 4 + j
            act.wait_ge(drained_v, i * 4 + (drain_base["f2_down2"] + j + 1))
            nc.scalar.activation(tile(actH, m), tile(x, m), ACT.Identity, scale=modc[:, bass.ds(m + 8, 1)],
                                 bias=modc[:, bass.ds(m, 1)]).then_inc(act_hi, 1)

        for n in range(len(PARTS)):
            slabs(f"f2_up{n}", 0, silu(f"f2_up{n}"))
            slabs(f"f2_down{n}", 0, nothing if n < 2 else modulated)
        for g in range(3):
            slabs(f"proj{g}", 0, nothing)

        def gate(i, j):
            act.wait_ge(slab_done, i * 4 + (stage_of["gates"]["base"] + j + 1))
            nc.scalar.activation(tile(gates, i * 4 + j), bank(j), ACT.Sigmoid,
                                 bias=col("b_gate", i * 4 + j)).then_inc(drained_a, 1)

        def turned_high(n):
            act.wait_ge(q2_T, max(n, 1) + 1)
            src, high, _, copy = turned(n)
            nc.scalar.activation(high, src, ACT.Copy).then_inc(q2_hi, 1)
            if copy is not None:
                nc.scalar.activation(copy, src, ACT.Copy).then_inc(k2_hi, 1)

        def gate_and_keys(i, j):
            gate(i, j)
            if isinstance(i, int) and j in (1, 2):
                turned_high(2 * j - 2)
                turned_high(2 * j - 1)

        slabs("gates", 0, gate_and_keys)
        for n in range(4, len(TURNS2)):
            turned_high(n)
        attention(group2, len(group1), prob2, probT2)
        for k in range(KT):
            act.wait_ge(at_T, 4 + k + 1)
            nc.scalar.activation(tile(actH, k), bank(k), ACT.Copy).then_inc(at_hi, 1)
        slabs("merge", 0, nothing)

        def ln_squares(n, ks):
            for k in ks:
                act.wait_ge(centred, n * KT + k + 1)
                if k >= 2:
                    act.wait_ge(*((acc_done, ACC_TOTAL[2] + SUMMED[k - 2]) if n == 0 else (sq_summed, k - 1)))
                nc.scalar.activation(tile(sq2, k % 2), tile(dev, k % 2), ACT.Square).then_inc(sq_ready, 1)

        def ln_drain(n):
            return lambda i, j: ln_squares(n, SQUARES_IN_SLAB[j]) if i == 1 else None

        slabs("out2", 0, ln_drain(0))
        ln_squares(0, (7,))
        for k in range(KT):
            act.wait_ge(scaled, k + 1)
            if k >= 2:
                act.wait_ge(act_ready, 5 * KT + k - 1)
            for into, done in ((tile(dev, k % 2), shifted), (tile(actH, k), act_hi)):
                nc.scalar.activation(into, tile(x, k), ACT.Identity, scale=ln_col[:, k:k + 1],
                                     bias=ln_col[:, KT + k:KT + k + 1]).then_inc(done, 1)

        def conv(name, n0):
            def drain(i, j):
                chan = i * 2 + (PARTS[n0][0] + j // 2 + (NF if j % 2 else 0))
                buf = (cg, cu)[j % 2][:, (j // 2) * S:(j // 2 + 1) * S]
                act.wait_ge(slab_done, i * 4 + (stage_of[name]["base"] + j + 1))
                act.wait_ge(hid_ready, i * 2 + (2 * (NF + KT) + PARTS[n0][0] + j // 2 - 1))
                nc.scalar.activation(buf, bank(j), ACT.Identity, scale=col("conv_w1", chan),
                                     bias=col("conv_b", chan)).then_inc(conv_c, 1)
                if j % 2:
                    gbuf = cg[:, (j // 2) * S:(j // 2 + 1) * S]
                    act.wait_ge(drained_v, i * 4 + (drain_base[name] + j))
                    nc.scalar.activation(gbuf, gbuf, ACT.Silu).then_inc(silu_ready, 1)
            return drain

        for n in range(len(PARTS)):
            slabs(f"f3_up{n}", 0, conv(f"f3_up{n}", n))
            slabs(f"f3_down{n}", 0, nothing if n < 2 else ln_drain(1))
        ln_squares(1, (7,))
        act.wait_ge(rn_ready, 5)
        for n in range(2 * ST):
            q = n % ST
            act.wait_ge(fin_T, n + 1)
            nc.scalar.activation(out_block(n), bank(FIN_BANK[n]), ACT.Identity, scale=rn[:, q:q + 1],
                                 bias=ln_mean[:, 3 * ST + q:3 * ST + q + 1]).then_inc(fin_norm, 1)

    @block.vector
    def _(dve):
        chain = Chain(dve, v_step)
        link = chain.link
        V = nc.vector

        def rsqrt(out, v, w, last=None):
            a = small[:, 64:64 + w]
            link(V.tensor_scalar(out.bitcast(I32), v.bitcast(I32), 1, None, ALU.logical_shift_right))
            link(V.tensor_scalar(out.bitcast(I32), out.bitcast(I32), -1.0, RSQRT_MAGIC, ALU.mult, ALU.add))
            for step in range(3):
                link(V.tensor_tensor(a, out, out, ALU.mult))
                link(V.scalar_tensor_tensor(a, a, -0.5, v, ALU.mult, ALU.mult))
                ins = V.scalar_tensor_tensor(out, a, 1.5, out, ALU.add, ALU.mult)
                if step == 2 and last is not None:
                    ins.then_inc(last[0], 1)
                    dve.wait_ge(*last)
                else:
                    link(ins)

        def row_scale(n, eps):
            dve.wait_ge(row_sum, n + 1)
            link(V.tensor_scalar(small[:, 0:ST], bank(4, ST), eps, None, ALU.add))
            rsqrt(rn[:], small[:, 0:ST], ST, last=(rn_ready, n + 1))
            dve.wait_ge(row_bcast, n + 1)
            V.tensor_copy(rB[:], bank(5)).then_inc(stat_out, 1)
            dve.wait_ge(stat_out, n + 1)

        def add_term(term, count):
            V.tensor_tensor(acc[:], acc[:], term, ALU.add).then_inc(acc_done, 1)
            dve.wait_ge(acc_done, count)

        for k in range(KT + 1):
            if k < KT:
                dve.wait_ge(xT, k + 1)
                V.tensor_copy(tile(x, k), bank(k % 4)).then_inc(drained_v, 1)
            if k:
                dve.wait_ge(drained_v, k)
                dve.wait_ge(act_hi, k)
                V.scalar_tensor_tensor(tile(actL, k - 1), tile(x, k - 1), gain0[:, k - 1:k],
                                       tile(actH, k - 1).bitcast(F32), ALU.mult, ALU.subtract).then_inc(act_ready, 1)
                dve.wait_ge(sq_ready, k)
                if k == 1:
                    V.tensor_copy(acc[:], sq[:]).then_inc(acc_done, 1)
                    dve.wait_ge(acc_done, 1)
                else:
                    add_term((sq, rB)[(k - 1) % 2][:], k)
        dve.wait_ge(vec_T, 1)
        V.tensor_copy(cols[:], bank(7)).then_inc(cols_ready, 1)
        dve.wait_ge(cols_ready, 1)
        dve.wait_ge(silu_c_ready, 2)
        row_scale(0, RMS_EPS)

        def mod_products(chunk, half, ctx_too):
            dve.wait_ge(mod_in[half], chunk * 16 + 16)
            n = 2 if ctx_too else 1
            for kk in range(4):
                w = mod_raw[:, (half * 4 + kk) * 512:][:, 0:512]
                for m in range(n):
                    k = half * 4 + kk
                    o, s = mod_acc[:, m * 512:(m + 1) * 512], silu_c[:, m * 8 + k:m * 8 + k + 1]
                    if k == 0:
                        ins = V.tensor_scalar(o, w, s, None, ALU.mult)
                    else:
                        ins = V.scalar_tensor_tensor(o, w, s, o, ALU.mult, ALU.add)
                    if kk < 3 or m < n - 1:
                        link(ins)
            ins.then_inc(mod_half, 1)
            dve.wait_ge(mod_half, chunk * 2 + (half + 1))

        def mod_columns(chunk, ctx_too):
            dve.wait_ge(mod_sum, chunk + 1)
            b = cols[:, bass.ds(chunk * 4 + VEC["b_mod"][1], 4)]
            if ctx_too:
                link(V.tensor_tensor(modx[:, bass.ds(chunk * 4, 4)], bank(6, 4, 4), b, ALU.add))
            V.tensor_tensor(modc[:, bass.ds(chunk * 4, 4)], bank(6, 4), b, ALU.add).then_inc(mod_cols, 1)
            dve.wait_ge(mod_cols, chunk + 1)

        def hidden(name, i, q, hid0):
            st, d0 = stage_of[name], drain_base[name]
            f = i * 2 + q
            dve.wait_ge(slab_done, i * 4 + (st["base"] + 2 * q + 1))
            V.tensor_tensor(g1[:], bank(2 * q), rB[:], ALU.mult).then_inc(drained_v, 1)
            dve.wait_ge(slab_done, i * 4 + (st["base"] + 2 * q + 2))
            V.tensor_tensor(ur[:], bank(2 * q + 1), rB[:], ALU.mult).then_inc(drained_v, 1)
            dve.wait_ge(drained_v, i * 4 + (d0 + 2 * q + 2))
            dve.wait_ge(silu_ready, f + (SILU_BEFORE[name] + 1))
            link(V.tensor_tensor(h[:], sg[:], ur[:], ALU.mult))
            link(V.tensor_scalar(tile(hidH, f), h[:], 1.0, None, ALU.mult))
            V.tensor_tensor(tile(hidL, f), h[:], tile(hidH, f).bitcast(F32), ALU.subtract).then_inc(hid_ready, 1)
            dve.wait_ge(hid_ready, f + (hid0 + 1))

        def add_down(name):
            st, d0 = stage_of[name], drain_base[name]

            def body(i):
                for j in range(SLOTS):
                    m = i * 4 + j
                    dve.wait_ge(slab_done, i * 4 + (st["base"] + j + 1))
                    V.scalar_tensor_tensor(tile(x, m), bank(j), 0.5, tile(x, m), ALU.mult, ALU.add).then_inc(drained_v, 1)
            chain.loop(0, 2, 0, body)
            dve.wait_ge(drained_v, d0 + KT)

        def last_down(name, scale, gain, act0, hi0, sq0, acc0):
            st, d0 = stage_of[name], drain_base[name]
            link(V.memset(acc[:], 0.0))

            def body(i):
                for j in range(SLOTS):
                    m = i * 4 + j
                    dve.wait_ge(slab_done, i * 4 + (st["base"] + j + 1))
                    V.scalar_tensor_tensor(tile(x, m), bank(j), scale, tile(x, m), ALU.mult, ALU.add).then_inc(drained_v, 1)
                    dve.wait_ge(drained_v, i * 4 + (d0 + j + 1))
                    dve.wait_ge(act_hi, i * 4 + (hi0 + j + 1))
                    V.scalar_tensor_tensor(tile(actL, m), tile(x, m), col(gain, m), tile(actH, m).bitcast(F32),
                                           ALU.mult, ALU.subtract).then_inc(act_ready, 1)
                    dve.wait_ge(sq_ready, i * 4 + (sq0 + j + 1))
                    add_term(sq[:], i * 4 + (acc0 + j + 1))
            chain.loop(0, 2, 0, body)
            dve.wait_ge(act_ready, act0 + KT)

        def context_operand():
            dve.wait_ge(ctx_T, 1)
            for k in range(KT):
                hi, lo = (c[k // 4][:, (k % 4) * CTX:(k % 4 + 1) * CTX] for c in (hcH, hcL))
                V.tensor_scalar(h[:, (k % 2) * CTX:][:, 0:CTX], bank(4 + k // 2, CTX, (k % 2) * CTX), modx[:, 8 + k:9 + k],
                                modx[:, k:k + 1], ALU.mult, ALU.add).then_inc(ctx_drained, 1)
                dve.wait_ge(ctx_drained, k + 1)
                link(V.tensor_copy(hi, h[:, (k % 2) * CTX:][:, 0:CTX]))
                V.tensor_tensor(lo, h[:, (k % 2) * CTX:][:, 0:CTX], hi.bitcast(F32), ALU.subtract).then_inc(hc_ready, 1)
            dve.wait_ge(hc_ready, KT)

        for n, (f0, nf) in enumerate(PARTS):
            def body(i, n=n, f0=f0):
                hidden(f"f1_up{n}", i, 0, f0)
                if not (isinstance(i, int) and i == 0):
                    mod_columns(i - 1 + 4 * n, n == 0)
                mod_products(i + 4 * n, 0, n == 0)
                hidden(f"f1_up{n}", i, 1, f0)
                mod_products(i + 4 * n, 1, n == 0)
            if n == 2:
                link(V.tensor_scalar(modx[:, 8:16], modx[:, 8:16], 1.0, None, ALU.add))
                context_operand()
            body(0)
            chain.loop(1, nf // 2, 2 * ((7 if n == 0 else 3) + 2) + (1 if n == 0 else 0), body)
            mod_columns(nf // 2 - 1 + 4 * n, n == 0)
            if n == 2:
                mod_products(11, 0, False)
                mod_products(11, 1, False)
            if n < 2:
                add_down(f"f1_down{n}")
            else:
                last_down("f1_down2", 0.5, "mix_norm", KT, KT, KT, ACC_TOTAL[0])

        mod_columns(11, False)
        link(V.tensor_scalar(modc[:, 8:16], modc[:, 8:16], 1.0, None, ALU.add))
        link(V.tensor_scalar(modc[:, 32:40], modc[:, 32:40], 1.0, None, ALU.add))
        row_scale(1, RMS_EPS)

        dve.wait_ge(misc_in, MISC_DMAS * 16)
        kc = kctx[:].rearrange("p (n d) -> p n d", n=4)
        for g, v in ((0, vA), (1, vB)):
            dve.wait_ge(slab_done, stage_of["ctxkv"]["base"] + 2 * g + 2)
            for q in range(CT):
                b = 2 * g + q
                link(V.tensor_tensor(kc[:, b, :], bank(b, P), biasx[:, g * 256:g * 256 + P], ALU.add))
                V.tensor_tensor(v[:, q * P:(q + 1) * P], bank(b, P, P), biasx[:, g * 256 + P:g * 256 + 256],
                                ALU.add).then_inc(drained_v, 1)
        dve.wait_ge(drained_v, drain_base["ctxkv"] + 4)
        kb = kctx[:, 2 * P:4 * P].rearrange("p (n d) -> p n d", d=DH)
        tk = tA[:, 0:2 * P].rearrange("p (n d) -> p n d", d=DH)
        link(V.tensor_tensor(tk, kb, kb, ALU.mult))
        link(V.tensor_reduce(small[:, 0:4], tk, AX_X, ALU.add))
        link(V.tensor_scalar(small[:, 0:4], small[:, 0:4], 1.0 / DH, QK_EPS, ALU.mult, ALU.add))
        rsqrt(small[:, 128:132], small[:, 0:4], 4)
        link(V.tensor_tensor(kb, kb, small[:, 128:132].unsqueeze(2).broadcast_to([P, 4, DH]), ALU.mult))
        V.tensor_tensor(kb, kb, gain2[:, DH:].unsqueeze(1).broadcast_to([P, 4, DH]), ALU.mult).then_inc(kctx_ready, 2)
        dve.wait_ge(kctx_ready, 2)
        link(V.tensor_scalar(sink[:, NH:], sink[:, 0:NH], -1.0, None, ALU.mult))

        def gained_tables(cos, sin, gain, groups, half):
            for n in range(2):
                g = gain[:, n * DH:(n + 1) * DH]
                c = ropeT[:, 2 * n * ST * DH:][:, 0:ST * DH].rearrange("p (q d) -> p q d", q=ST)
                s = ropeT[:, (2 * n + 1) * ST * DH:][:, 0:ST * DH].rearrange("p (q d) -> p q d", q=ST)
                link(V.tensor_tensor(c, cos.rearrange("p (q d) -> p q d", q=ST),
                                     g.unsqueeze(1).broadcast_to([P, ST, DH]), ALU.mult))
                for r in range(groups):
                    for to, frm in ((0, half), (half, 0)):
                        a = 2 * r * half
                        link(V.tensor_tensor(s[:, :, a + to:a + to + half],
                                             sin.rearrange("p (q d) -> p q d", q=ST)[:, :, a + to:a + to + half],
                                             g[:, a + frm:a + frm + half].unsqueeze(1).broadcast_to([P, ST, half]),
                                             ALU.mult))

        dve.wait_ge(tables_in, 16)
        gained_tables(cv("cos1"), cv("sin1"), gain1, 1, DH // 2)

        for q in range(ST):
            dve.wait_ge(drained_a, drain_base["idx"] + q + 1)
            v = pi[:, q * IDX_COLS:][:, 0:(IDX_HEADS + 1) * IDX_DIM].rearrange("p (h d) -> p h d", d=IDX_DIM)[:, :, 0:IDX_ROT]
            tmp = tA[:, 0:(IDX_HEADS + 1) * IDX_ROT].rearrange("p (h d) -> p h d", d=IDX_ROT)
            rotate(V, link, v, tmp, IDX_HEADS + 1, 1, IDX_ROT // 2, cv("cosi")[:, q * IDX_ROT:(q + 1) * IDX_ROT],
                 cv("sini")[:, q * IDX_ROT:(q + 1) * IDX_ROT], last=idx_rot)
            dve.wait_ge(idx_rot, q + 1)
        wi = pi[:].rearrange("p (q c) -> p q c", q=ST)[:, :, IDX_COLS - IDX_HEADS:]
        link(V.tensor_scalar(wi, wi, IDX_SCALE, None, ALU.mult))
        dve.wait_ge(idx_T, 1)
        for dst, src in ((qiT[:, 0:S], bank(4)), (qiT[:, S:], bank(5)), (kiT[0:DH, :], ps[0:DH, 6, :]),
                         (kiT[DH:P, :], ps[0:DH, 6, :])):
            V.tensor_copy(dst, src).then_inc(idx_cols, 1)

        def mask_of(q):
            return work[:, P * (q * (q + 1) // 2 - 1):][:, 0:P * (q + 1)]

        for n in range((ST - 1) * IDX_HEADS):
            q, head = n // IDX_HEADS + 1, n % IDX_HEADS
            w, m = P * (q + 1), mask_of(q)
            r, c = rel[:, (n % 2) * S:][:, 0:w], pi[:, q * IDX_COLS + IDX_COLS - IDX_HEADS + head:][:, 0:1]
            dve.wait_ge(idx_rel, n + 1)
            if head == 0:
                V.tensor_scalar(m, r, c, None, ALU.mult).then_inc(idx_rel_used, 1)
            else:
                V.scalar_tensor_tensor(m, r, c, m, ALU.mult, ALU.add).then_inc(idx_rel_used, 1)
            dve.wait_ge(idx_rel_used, n + 1)
            if head == IDX_HEADS - 1:
                link(V.tensor_tensor(m[:, q * P:], m[:, q * P:], cv("causal"), ALU.add))

        def pick(q, first=0, end=TOPK // 8):
            m, top = mask_of(q), small[:, 0:8]
            for _ in range(first, end):
                link(V.max(top, m))
                link(V.match_replace(m, top, m, TAKEN))
            if end == TOPK // 8:
                link(V.tensor_scalar(m, m, TAKEN / 1.5, NEG, ALU.is_gt, ALU.mult))

        pick(1)

        pick(2)

        def head_scales(n, out, last=None):
            dve.wait_ge(qk_sq, n + 1)
            link(V.tensor_scalar(small[:, 0:32], ssq[:, n * 32:n * 32 + 32], 1.0 / DH, RMS_EPS, ALU.mult, ALU.add))
            rsqrt(out, small[:, 0:32], 32, last=last)

        head_scales(0, small[:, 128:160])
        heads_rotated(V, chain, q1, 0, tA, small[:, 128:160], qk_rot)
        head_scales(1, k_scale[:], last=(k_scaled, 1))
        pick(3, 0, 5)
        for g in range(4):
            dve.wait_ge(pool_hi, g + 1)
            V.scalar_tensor_tensor(tile(hidL, 4 + g), bank(4 + g), col("pool_scale", g), tile(hidH, 4 + g).bitcast(F32),
                                   ALU.mult, ALU.subtract).then_inc(hid_ready, 1)

        pick(3, 5)

        def attention(units, n0, prob, probT):
            def logits(n):
                u, c = units[n - n0], n % 32
                dve.wait_ge(att_qk, n + 1)
                if n >= 3:
                    dve.wait_ge(prob_T, n - 2)
                b = 2 * (n % 2)
                src = ps[:, b:b + 2, :].rearrange("p b n -> p (b n)")[:, u["col0"]:u["col0"] + u["W"]]
                start = 3e38 if u["sink"] is None else sink[:, NH + u["sink"]:][:, 0:1]
                V.tensor_tensor_reduce(out=prob[:, (n % 3) * 768:][:, 0:u["W"]], in0=src, in1=u["mask"],
                                       scale=-(DH ** -0.5), scalar=start, op0=ALU.add, op1=ALU.min,
                                       accum_out=stat[:, c:c + 1]).then_inc(logit, 1)

            def sums(n):
                u, c = units[n - n0], n % 32
                dve.wait_ge(probs, n + 1)
                total = stat[:, 32 + c:33 + c]
                if u["sink"] is not None:
                    link(V.tensor_tensor(total, total, stat[:, 64 + c:65 + c], ALU.add))
                link(V.reciprocal(stat[:, 96 + c:97 + c], total))

            def copy(n):
                u = units[n - n0]
                if u["W"] > 512:
                    dve.wait_ge(prob_T, n + 1)
                    dve.wait_ge(pv, n - 1)
                    V.tensor_copy(probT[:, (n % 2) * 768 + 512:][:, 0:u["W"] - 512],
                                  bank(5, u["W"] - 512)).then_inc(probT_v, 1)

            def out(n):
                u, c = units[n - n0], n % 32
                dve.wait_ge(pv, n + 1)
                V.tensor_scalar(u["out"], bank(6 + n % 2, DH), stat[:, 96 + c:97 + c], None, ALU.mult).then_inc(attn_out, 1)

            end = n0 + len(units)
            logits(n0)
            logits(n0 + 1)
            for n in range(n0, end):
                copy(n)
                if n + 2 < end:
                    logits(n + 2)
                sums(n)
                if n > n0:
                    out(n - 1)
            out(end - 1)

        attention(group1, 0, prob1, probT1)
        for k in range(4):
            dve.wait_ge(at_hi, k + 1)
            V.tensor_tensor(tile(hidL, k), bank(k), tile(hidH, k).bitcast(F32), ALU.subtract).then_inc(hid_ready, 1)
        last_down("out1", 1.0, "ffn2_norm", 2 * KT, 2 * KT, 2 * KT, ACC_TOTAL[1])
        row_scale(2, RMS_EPS)

        for n, (f0, nf) in enumerate(PARTS):
            chain.loop(0, nf // 2, 4, lambda i, n=n, f0=f0: [hidden(f"f2_up{n}", i, q, NF + KT + f0) for q in range(2)])
            if n < 2:
                add_down(f"f2_down{n}")
        st, d0 = stage_of["f2_down2"], drain_base["f2_down2"]

        def modulated(i):
            for j in range(SLOTS):
                m = i * 4 + j
                dve.wait_ge(slab_done, i * 4 + (st["base"] + j + 1))
                V.scalar_tensor_tensor(tile(x, m), bank(j), 0.5, tile(x, m), ALU.mult, ALU.add).then_inc(drained_v, 1)
                dve.wait_ge(drained_v, i * 4 + (d0 + j + 1))
                link(V.tensor_scalar(h[:], tile(x, m), modc[:, bass.ds(m + 8, 1)], modc[:, bass.ds(m, 1)],
                                     ALU.mult, ALU.add))
                dve.wait_ge(act_hi, i * 4 + (3 * KT + j + 1))
                V.tensor_tensor(tile(actL, m), h[:], tile(actH, m).bitcast(F32), ALU.subtract).then_inc(act_ready, 1)
                dve.wait_ge(act_ready, i * 4 + (3 * KT + j + 1))
        chain.loop(0, 2, 4, modulated)
        gained_tables(cv("cos2"), cv("sin2"), gain2, 2, DH // 4)

        dve.wait_ge(bias_in, 16)
        for g in range(3):
            dve.wait_ge(slab_done, stage_of[f"proj{g}"]["base"] + SLOTS)
            for q in range(ST):
                V.tensor_tensor(nat[:, q * 1536 + g * 512:][:, 0:512], bank((4, 0, 4)[g] + q),
                                bias2[:, g * 512:(g + 1) * 512], ALU.add).then_inc(drained_v, 1)
        dve.wait_ge(drained_v, drain_base["merge"])
        HB = NH + NKV
        for q in range(ST):
            a = q * 1536
            xa = nat[:, a:a + HB * DH].rearrange("p (h d) -> p h d", d=DH)
            tmp = tC[:, 0:HB * DH].rearrange("p (h d) -> p h d", d=DH)
            rotate(V, link, xa, tmp, HB, 2, DH // 4, cv("cos2")[:, q * DH:(q + 1) * DH], cv("sin2")[:, q * DH:(q + 1) * DH])
            xb = nat[:, a + 768:a + 768 + HB * DH].rearrange("p (h d) -> p h d", d=DH)
            link(V.tensor_tensor(tmp, xb, xb, ALU.mult))
            link(V.tensor_reduce(ssq[:, q * HB:(q + 1) * HB], tmp, AX_X, ALU.add))
            link(V.tensor_copy(vA[:, (CT + q) * P:(CT + q + 1) * P], nat[:, a + 640:a + 768]))
            link(V.tensor_copy(vB[:, (CT + q) * P:(CT + q + 1) * P], nat[:, a + 1408:a + 1536]))
        link(V.tensor_scalar(small[:, 0:ST * HB], ssq[:, 0:ST * HB], 1.0 / DH, QK_EPS, ALU.mult, ALU.add))
        rsqrt(small[:, 128:128 + ST * HB], small[:, 0:ST * HB], ST * HB)
        for q in range(ST):
            a = q * 1536 + 768
            xb = nat[:, a:a + HB * DH].rearrange("p (h d) -> p h d", d=DH)
            link(V.tensor_tensor(xb, xb, small[:, 128 + q * HB:][:, 0:HB].unsqueeze(2).broadcast_to([P, HB, DH]),
                                 ALU.mult))
            for n, first, heads in ((0, 0, NH), (1, NH, NKV)):
                last = q2_rot if q == ST - 1 and n == 1 else None
                rotate(V, link, xb[:, first:first + heads, :], tC[:, 0:heads * DH].rearrange("p (h d) -> p h d", d=DH),
                     heads, 2, DH // 4, gained(n, 0, q), gained(n, 1, q), last=last)
        for n in range(len(TURNS2)):
            src, high, low, copy = turned(n)
            dve.wait_ge(q2_hi, n + 1)
            if copy is not None:
                dve.wait_ge(k2_hi, n + 1)
            V.tensor_tensor(low, src, high.bitcast(F32), ALU.subtract).then_inc(q2_lo, 1)
        dve.wait_ge(q2_lo, len(TURNS2))

        attention(group2, len(group1), prob2, probT2)
        for k in range(KT):
            dve.wait_ge(at_hi, 4 + k + 1)
            V.tensor_tensor(tile(actL, k), bank(k), tile(actH, k).bitcast(F32), ALU.subtract).then_inc(act_ready, 1)

        def merge(i):
            for j in range(SLOTS):
                m = i * 4 + j
                dve.wait_ge(slab_done, i * 4 + (stage_of["merge"]["base"] + j + 1))
                link(V.tensor_tensor(mA[:], bank(j), tile(gates, m), ALU.mult))
                V.tensor_tensor(mB[:], bank(4 + j), tile(gates, m + 8), ALU.mult).then_inc(drained_v, 1)
                dve.wait_ge(drained_v, i * 4 + (drain_base["merge"] + j + 1))
                link(V.tensor_tensor(mA[:], mA[:], mB[:], ALU.add))
                link(V.tensor_scalar(tile(hidH, m), mA[:], 1.0, None, ALU.mult))
                V.tensor_tensor(tile(hidL, m), mA[:], tile(hidH, m).bitcast(F32), ALU.subtract).then_inc(hid_ready, 1)
                dve.wait_ge(hid_ready, i * 4 + (2 * NF + KT + j + 1))
        chain.loop(0, 2, 12, merge)

        def residual_tile(name, i, j, gate0, buf, scale):
            m = i * 4 + j
            dve.wait_ge(slab_done, i * 4 + (stage_of[name]["base"] + j + 1))
            V.tensor_scalar(buf[:], bank(j), modc[:, bass.ds(m + gate0, 1)], None, ALU.mult).then_inc(drained_v, 1)
            dve.wait_ge(drained_v, i * 4 + (drain_base[name] + j + 1))
            link(V.scalar_tensor_tensor(tile(x, m), tile(x, m), scale, buf[:], ALU.mult, ALU.add))

        def residual(name, gate0, buf, scale):
            chain.loop(0, 2, 4, lambda i: [residual_tile(name, i, j, gate0, buf, scale) for j in range(SLOTS)])

        def residual_norm(n, name, gate0, buf, scale):
            before, base = ACC_TOTAL[2 + n], 3 * KT + n * KT
            mu, c, md, shift = (ln_mean[:, g * ST:(g + 1) * ST] for g in range(4))
            link(V.memset(acc[:], 0.0))
            for what, k in LN_STEPS:
                if what in "xu":
                    residual_tile(name, k // 4, k % 4, gate0, buf, scale)
                if what in "xa":
                    before += 1
                    add_term(tile(x, k), before)
                if what == "c":
                    dve.wait_ge(mean_sum, n + 1)
                    if n == 0:
                        link(V.memset(sq[:], 0.0))
                    link(V.tensor_scalar(c, ps[:, 5, 8:8 + ST], 2.0, None, ALU.mult))
                    link(V.tensor_scalar(rB[:], bank(4), 2.0, None, ALU.mult))
                if what == "d":
                    if k >= 2:
                        dve.wait_ge(sq_ready, base + k - 1)
                    V.tensor_tensor(tile(dev, k % 2), tile(x, k), rB[:], ALU.subtract).then_inc(centred, 1)
                if what == "s" and n == 0:
                    before += 1
                    dve.wait_ge(sq_ready, base + k + 1)
                    V.tensor_tensor(sq[:], sq[:], tile(sq2, k % 2), ALU.add).then_inc(acc_done, 1)
                    dve.wait_ge(acc_done, before)
            dve.wait_ge(row_sum, 4 + n)
            link(V.tensor_copy(mu, ps[:, 5, 0:ST]))
            link(V.tensor_tensor(md, mu, c, ALU.subtract))
            link(V.tensor_tensor(md, md, md, ALU.mult))
            link(V.scalar_tensor_tensor(small[:, 0:ST], ps[:, 5, 4:4 + ST], LN_EPS, md, ALU.add, ALU.subtract))
            rsqrt(rn[:], small[:, 0:ST], ST)
            V.scalar_tensor_tensor(shift, mu, -1.0, rn[:], ALU.mult, ALU.mult).then_inc(rn_ready, 1)
            dve.wait_ge(rn_ready, 4 + n)

        residual_norm(0, "out2", 16, mA, ALPHA)
        s2 = modc[:, 32:40]
        g0, b0 = (cols[:, VEC[n][1]:VEC[n][1] + KT] for n in ("ln1_g", "ln1_b"))
        link(V.tensor_tensor(ln_col[:, 0:KT], g0, s2, ALU.mult))
        link(V.tensor_tensor(ln_col[:, KT:], b0, s2, ALU.mult))
        link(V.tensor_tensor(ln_col[:, KT:], ln_col[:, KT:], modc[:, 24:32], ALU.add))
        dve.wait_ge(row_bcast, 4)
        for k in range(KT + 1):
            if k < KT:
                link(V.tensor_tensor(tile(x, k), tile(x, k), bank(7), ALU.subtract))
                V.tensor_tensor(tile(x, k), tile(x, k), bank(6), ALU.mult).then_inc(scaled, 1)
            if k:
                dve.wait_ge(shifted, k)
                dve.wait_ge(act_hi, 4 * KT + k)
                V.tensor_tensor(tile(actL, k - 1), tile(dev, (k - 1) % 2), tile(actH, k - 1).bitcast(F32),
                                ALU.subtract).then_inc(act_ready, 1)
        dve.wait_ge(scaled, KT)
        for k in range(KT):
            link(V.tensor_scalar(tile(x, k), tile(x, k), col("ln1_g", k), col("ln1_b", k), ALU.mult, ALU.add))

        def conv(i, n):
            name, (f0, nf) = f"f3_up{n}", PARTS[n]
            s, d = stage_of[name], drain_base[name]
            before = 2 * f0
            for j in range(SLOTS):
                chan = i * 2 + (f0 + j // 2 + (NF if j % 2 else 0))
                buf = (cg, cu)[j % 2][:, (j // 2) * S:(j // 2 + 1) * S]
                dve.wait_ge(conv_c, i * 4 + (before + j + 1))
                link(V.scalar_tensor_tensor(buf[:, 1:S], bank(j, S - 1), col("conv_w0", chan), buf[:, 1:S],
                                            ALU.mult, ALU.add))
                V.scalar_tensor_tensor(buf[:, 0:S - 1], bank(j, S - 1, 1), col("conv_w2", chan), buf[:, 0:S - 1],
                                       ALU.mult, ALU.add).then_inc(drained_v, 1)
                if j % 2:
                    q = j // 2
                    dve.wait_ge(drained_v, i * 4 + (d + j + 1))
                    dve.wait_ge(silu_ready, i * 2 + (2 * NF + f0 + q + 1))
                    link(V.tensor_tensor(h3[:], cg[:, q * S:(q + 1) * S], buf, ALU.mult))
                    link(V.tensor_scalar(tile(hidH, i * 2 + q), h3[:], 1.0, None, ALU.mult))
                    V.tensor_tensor(tile(hidL, i * 2 + q), h3[:], tile(hidH, i * 2 + q).bitcast(F32),
                                    ALU.subtract).then_inc(hid_ready, 1)
                    dve.wait_ge(hid_ready, i * 2 + (2 * (NF + KT) + f0 + q + 1))

        for n, (f0, nf) in enumerate(PARTS):
            chain.loop(0, nf // 2, 8, lambda i, n=n: conv(i, n))
            if n < 2:
                residual(f"f3_down{n}", 40, h3, ALPHA if n == 0 else 1.0)
            else:
                residual_norm(1, "f3_down2", 40, h3, 1.0)

        dve.wait_ge(gb_in, 32)
        for n in BY_V:
            o, half = out_block(n), n // ST
            dve.wait_ge(fin_norm, n + 1)
            link(V.tensor_tensor(o, o, ln2_gB[:, half * 512:half * 512 + 512], ALU.mult))
            V.tensor_tensor(o, o, ln2_bB[:, half * 512:half * 512 + 512], ALU.add).then_inc(fin_v, 1)


_NAMES = ["x", "ffn1_norm", "ffn1_w_gate", "ffn1_w_up", "ffn1_w_down", "mix_norm", "w_in", "q_norm", "k_norm",
          "pool_w", "pool_scale", "w_out", "ffn2_norm", "ffn2_w_gate", "ffn2_w_up", "ffn2_w_down", "c_2", "ctx_2",
          "c_ctx_2", "w_mod_2", "b_mod_2", "w_in_2", "b_in_2", "attn_sink_2", "q_norm_g_2", "k_norm_g_2",
          "w_branch_a_2", "w_branch_b_2", "w_out_2", "ln1_g_2", "ln1_b_2", "w_up_2", "conv_w_2", "conv_b_2",
          "w_down_2", "ln2_g_2", "ln2_b_2"]


def kernel(**inputs):
    import concourse.bacc as bacc
    from concourse.bass_utils import run_bass_kernel_spmd

    nc = bacc.Bacc("TRN2", target_bir_lowering=False, num_devices=1)
    arrays, t = {}, {}
    for name in _NAMES:
        a = np.ascontiguousarray(inputs[name])
        arrays[f"in_{name}"] = a
        t[name] = nc.dram_tensor(f"in_{name}", a.shape, mybir.dt.from_np(a.dtype), kind="ExternalInput").ap()
    arrays["in_const"] = constants()
    t["const"] = nc.dram_tensor("in_const", (P, N_CONST), F32, kind="ExternalInput").ap()
    t["out"] = nc.dram_tensor("out_0", (1, S, D), F32, kind="ExternalOutput").ap()
    build(nc, t)
    r = run_bass_kernel_spmd(nc, [arrays], core_ids=[0])
    return r.results[0]["out_0"]
```
